# Optimizing a Trainium2 kernel written in Bass

```python
import math
import jax
import jax.numpy as jnp
from jax import lax
import numpy as np

D_MODEL = 1024
BATCH = 1
SEQ = 256
DEPTH = 2
DEC_BATCH = 8
DEC_SEQ = 8
PAST_LEN = 2048
PAGE_SIZE = 128

N_META = 16
GDN_HEADS = 4
GDN_DK = 128
GDN_DV = 128
GDN_QK_W = GDN_HEADS * GDN_DK
GDN_V_W = GDN_HEADS * GDN_DV
GDN_CONV = 4
GDN_CONV_CH = 2 * GDN_QK_W + GDN_V_W
CHUNK = 64
SC_CH = D_MODEL - GDN_V_W
SC_CONV = 3
D_FF = 2816
NORM_EPS = 1e-6
L2_EPS = 1e-6

OFF_Q = 0
OFF_K = OFF_Q + GDN_QK_W
OFF_V = OFF_K + GDN_QK_W
OFF_Z = OFF_V + GDN_V_W
OFF_BETA = OFF_Z + GDN_V_W
OFF_A = OFF_BETA + GDN_HEADS
OFF_B = OFF_A + GDN_HEADS
OFF_C = OFF_B + SC_CH
OFF_H = OFF_C + SC_CH
PROJ_W = OFF_H + SC_CH

kernel_name = "hymba_gdn_shortconv_macaron_step"

def rms_norm(x, gain):
    xf = x.astype(jnp.float32)
    y = xf * lax.rsqrt(jnp.mean(xf * xf, axis=-1, keepdims=True) + NORM_EPS)
    return (y * gain.astype(jnp.float32)).astype(x.dtype)

def l2_normalize(x):
    return x * lax.rsqrt(jnp.sum(x * x, axis=-1, keepdims=True) + L2_EPS)

def causal_dw_conv(x_ext, w):
    width = w.shape[0]
    t = x_ext.shape[1] - width + 1
    out = x_ext[:, 0:t] * w[0]
    for i in range(1, width):
        out = out + x_ext[:, i:i + t] * w[i]
    return out

def swiglu(x, w_gate, w_up, w_down):
    return (jax.nn.silu(x @ w_gate) * (x @ w_up)) @ w_down

def gdn_chunks(q, k, v, beta, g, s0, chunk):
    bsz, t, h, _ = q.shape
    n = t // chunk

    def blocks(a):
        return jnp.moveaxis(a.reshape((bsz, n, chunk) + a.shape[2:]), 3, 1)

    qb, kb, vb, bb, gb = blocks(q), blocks(k), blocks(v), blocks(beta), blocks(g)
    G = jnp.cumsum(gb, axis=-1)
    idx = jnp.arange(chunk)
    strict = idx[:, None] > idx[None, :]
    incl = idx[:, None] >= idx[None, :]
    diff = G[..., :, None] - G[..., None, :]
    d_strict = jnp.exp(jnp.where(strict, diff, -jnp.inf))
    d_incl = jnp.exp(jnp.where(incl, diff, -jnp.inf))
    kk = jnp.einsum('bhnid,bhnjd->bhnij', kb, kb)
    tmat = bb[..., :, None] * kk * d_strict + jnp.eye(chunk, dtype=jnp.float32)
    u = lax.linalg.triangular_solve(tmat, bb[..., None] * vb, left_side=True, lower=True)
    w = lax.linalg.triangular_solve(tmat, (bb * jnp.exp(G))[..., None] * kb, left_side=True, lower=True)
    qk = jnp.einsum('bhnid,bhnjd->bhnij', qb, kb) * d_incl
    q_dec = qb * jnp.exp(G)[..., None]
    k_tail = kb * jnp.exp(G[..., -1:] - G)[..., None]
    e_last = jnp.exp(G[..., -1])
    xs = tuple(jnp.moveaxis(a, 2, 0) for a in (q_dec, k_tail, u, w, qk, e_last))

    def step(s, inp):
        qd, kt, uc, wc, qkc, el = inp
        nv = uc - jnp.einsum('bhlk,bhkv->bhlv', wc, s)
        o = jnp.einsum('bhlk,bhkv->bhlv', qd, s) + jnp.einsum('bhij,bhjv->bhiv', qkc, nv)
        s = el[..., None, None] * s + jnp.einsum('bhlk,bhlv->bhkv', kt, nv)
        return s, o

    s, o = lax.scan(step, s0, xs)
    o = jnp.transpose(o, (1, 0, 3, 2, 4)).reshape(bsz, t, h, o.shape[-1])
    return o, s

def mixer(h, conv_gdn_buf, sconv_buf, s0, segments, w_in, w_out, conv_gdn, conv_sc, a_log, dt_bias, gdn_norm):
    bsz, t, _ = h.shape
    f32 = jnp.float32
    proj = h @ w_in
    qkv = proj[..., OFF_Q:OFF_Z]
    z = proj[..., OFF_Z:OFF_BETA]
    b_raw = proj[..., OFF_BETA:OFF_A]
    a_raw = proj[..., OFF_A:OFF_B]
    gate_b = proj[..., OFF_B:OFF_C]
    gate_c = proj[..., OFF_C:OFF_H]
    h_in = proj[..., OFF_H:PROJ_W]

    qkv_ext = jnp.concatenate([conv_gdn_buf.astype(qkv.dtype), qkv], axis=1)
    new_conv_gdn = qkv_ext[:, qkv_ext.shape[1] - (GDN_CONV - 1):]
    qkv = jax.nn.silu(causal_dw_conv(qkv_ext, conv_gdn)).astype(f32)
    q = l2_normalize(qkv[..., :GDN_QK_W].reshape(bsz, t, GDN_HEADS, GDN_DK)) * (GDN_DK ** -0.5)
    k = l2_normalize(qkv[..., GDN_QK_W:2 * GDN_QK_W].reshape(bsz, t, GDN_HEADS, GDN_DK))
    v = qkv[..., 2 * GDN_QK_W:].reshape(bsz, t, GDN_HEADS, GDN_DV)
    beta = jax.nn.sigmoid(b_raw.astype(f32))
    g = -jnp.exp(a_log.astype(f32)) * jax.nn.softplus(a_raw.astype(f32) + dt_bias.astype(f32))
    s = s0.astype(f32)
    outs = []
    start = 0
    for length, chunk in segments:
        sl = slice(start, start + length)
        o_seg, s = gdn_chunks(q[:, sl], k[:, sl], v[:, sl], beta[:, sl], g[:, sl], s, chunk)
        outs.append(o_seg)
        start += length
    o = jnp.concatenate(outs, axis=1) if len(outs) > 1 else outs[0]
    o = o * lax.rsqrt(jnp.mean(o * o, axis=-1, keepdims=True) + NORM_EPS) * gdn_norm.astype(f32)
    o = o * jax.nn.silu(z.astype(f32).reshape(bsz, t, GDN_HEADS, GDN_DV))
    o = o.reshape(bsz, t, GDN_V_W).astype(h.dtype)

    u = gate_c * h_in
    u_ext = jnp.concatenate([sconv_buf.astype(u.dtype), u], axis=1)
    new_sconv = u_ext[:, u_ext.shape[1] - (SC_CONV - 1):]
    y_sc = gate_b * causal_dw_conv(u_ext, conv_sc)

    out = jnp.concatenate([o, y_sc], axis=-1) @ w_out
    return out, s, new_conv_gdn, new_sconv

def trunk(x, state_gdn, cache_gdn_conv, cache_sconv, segments, w_in, w_out, conv_gdn, conv_sc,
          a_log, dt_bias, gdn_norm, norm_gains, ffn1_gate, ffn1_up, ffn1_down, ffn2_gate, ffn2_up, ffn2_down):
    states, convs, sconvs = [], [], []
    for l in range(DEPTH):
        ng = norm_gains[l]
        x = x + 0.5 * rms_norm(swiglu(rms_norm(x, ng[0]), ffn1_gate[l], ffn1_up[l], ffn1_down[l]), ng[1])
        mix, s, cg, cs = mixer(rms_norm(x, ng[2]), cache_gdn_conv[l], cache_sconv[l], state_gdn[l], segments,
                               w_in[l], w_out[l], conv_gdn[l], conv_sc[l], a_log[l], dt_bias[l], gdn_norm[l])
        x = x + rms_norm(mix, ng[3])
        x = x + 0.5 * rms_norm(swiglu(rms_norm(x, ng[4]), ffn2_gate[l], ffn2_up[l], ffn2_down[l]), ng[5])
        states.append(s)
        convs.append(cg)
        sconvs.append(cs)
    return x, jnp.stack(states), jnp.stack(convs), jnp.stack(sconvs)

def setup_inputs(seed: int = 0) -> dict:
    key = jax.random.key(seed)
    ks = jax.random.split(key, 20)
    nrm = jax.random.normal
    dt = jnp.exp(jax.random.uniform(ks[9], (DEPTH, GDN_HEADS), minval=math.log(1e-3), maxval=math.log(1e-1)))
    return {
        "x_prompt": nrm(ks[0], (BATCH, SEQ, D_MODEL), jnp.float32),
        "x_sample": nrm(ks[1], (DEC_BATCH, DEC_SEQ, D_MODEL), jnp.float32),
        "state_gdn": 0.1 * nrm(ks[2], (DEPTH, DEC_BATCH, GDN_HEADS, GDN_DK, GDN_DV), jnp.float32),
        "cache_gdn_conv": nrm(ks[3], (DEPTH, DEC_BATCH, GDN_CONV - 1, GDN_CONV_CH), jnp.float32),
        "cache_sconv": nrm(ks[4], (DEPTH, DEC_BATCH, SC_CONV - 1, SC_CH), jnp.float32),
        "meta_tokens": nrm(ks[5], (N_META, D_MODEL), jnp.float32),
        "w_in": nrm(ks[6], (DEPTH, D_MODEL, PROJ_W), jnp.float32) * D_MODEL ** -0.5,
        "w_out": nrm(ks[7], (DEPTH, D_MODEL, D_MODEL), jnp.float32) * D_MODEL ** -0.5,
        "conv_gdn": nrm(ks[8], (DEPTH, GDN_CONV, GDN_CONV_CH), jnp.float32) * GDN_CONV ** -0.5,
        "conv_sc": nrm(ks[10], (DEPTH, SC_CONV, SC_CH), jnp.float32) * SC_CONV ** -0.5,
        "a_log": jnp.log(jax.random.uniform(ks[11], (DEPTH, GDN_HEADS), minval=1.0, maxval=16.0)),
        "dt_bias": dt + jnp.log(-jnp.expm1(-dt)),
        "gdn_norm": 1.0 + 0.01 * nrm(ks[12], (DEPTH, GDN_DV), jnp.float32),
        "norm_gains": 1.0 + 0.01 * nrm(ks[13], (DEPTH, 6, D_MODEL), jnp.float32),
        "ffn1_gate": nrm(ks[14], (DEPTH, D_MODEL, D_FF), jnp.float32) * D_MODEL ** -0.5,
        "ffn1_up": nrm(ks[15], (DEPTH, D_MODEL, D_FF), jnp.float32) * D_MODEL ** -0.5,
        "ffn1_down": nrm(ks[16], (DEPTH, D_FF, D_MODEL), jnp.float32) * D_FF ** -0.5,
        "ffn2_gate": nrm(ks[17], (DEPTH, D_MODEL, D_FF), jnp.float32) * D_MODEL ** -0.5,
        "ffn2_up": nrm(ks[18], (DEPTH, D_MODEL, D_FF), jnp.float32) * D_MODEL ** -0.5,
        "ffn2_down": nrm(ks[19], (DEPTH, D_FF, D_MODEL), jnp.float32) * D_FF ** -0.5,
    }

def reference(x_prompt, x_sample, state_gdn, cache_gdn_conv, cache_sconv, meta_tokens, w_in, w_out,
              conv_gdn, conv_sc, a_log, dt_bias, gdn_norm, norm_gains, ffn1_gate, ffn1_up, ffn1_down,
              ffn2_gate, ffn2_up, ffn2_down):
    weights = (w_in, w_out, conv_gdn, conv_sc, a_log, dt_bias, gdn_norm, norm_gains,
               ffn1_gate, ffn1_up, ffn1_down, ffn2_gate, ffn2_up, ffn2_down)
    bsz, seq, _ = x_prompt.shape
    meta = jnp.broadcast_to(meta_tokens.astype(x_prompt.dtype)[None], (bsz, N_META, D_MODEL))
    xp = jnp.concatenate([meta, x_prompt], axis=1)
    zero_state = jnp.zeros((DEPTH, bsz, GDN_HEADS, GDN_DK, GDN_DV), jnp.float32)
    zero_conv = jnp.zeros((DEPTH, bsz, GDN_CONV - 1, GDN_CONV_CH), x_prompt.dtype)
    zero_sconv = jnp.zeros((DEPTH, bsz, SC_CONV - 1, SC_CH), x_prompt.dtype)
    yp, state_p, conv_p, sconv_p = trunk(xp, zero_state, zero_conv, zero_sconv,
                                         ((N_META, N_META), (seq, CHUNK)), *weights)
    dec_seq = x_sample.shape[1]
    ys, state_s, conv_s, sconv_s = trunk(x_sample, state_gdn, cache_gdn_conv, cache_sconv,
                                         ((dec_seq, dec_seq),), *weights)
    y_prompt = yp[:, N_META:]
    return (y_prompt, ys, state_p.astype(state_gdn.dtype), conv_p, sconv_p,
            state_s.astype(state_gdn.dtype), conv_s, sconv_s)


_drawn_inputs = setup_inputs


def setup_inputs(seed=0):
    import zlib

    import numpy as np

    out = dict(_drawn_inputs(seed))
    spreads = {}
    factors = {}
    for name, (base, spread) in spreads.items():
        noise = np.random.default_rng([zlib.crc32(name.encode()), seed]).standard_normal(out[name].shape)
        drawn = base * np.exp(spread * noise) if base else spread * noise
        out[name] = jnp.asarray(drawn.astype(out[name].dtype))
    for name, factor in factors.items():
        out[name] = (out[name] * factor).astype(out[name].dtype)
    return out
```

```python
from contextlib import ExitStack

import numpy as np

import concourse.bass as bass
from concourse import mybir

F32 = mybir.dt.float32
F32R = mybir.dt.float32r
ALU = mybir.AluOpType
ACT = mybir.ActivationFunctionType

P = 128
DEPTH = 2
D_MODEL = 1024
KT = D_MODEL // P
HEADS = 4
N_PROMPT, N_META = 256, 16
SEQS, SEQ_T = 8, 8
N_SAMPLE = SEQS * SEQ_T
T = N_PROMPT + N_SAMPLE + N_META
TT = 3
TP = TT * P
C_TILE = 2
META_AT = N_SAMPLE
D_FF = 2816
FT = D_FF // P
DH = FT // 2
QKV_T = 12
GW, SW = 4, 3
EPS = 1e-6

G_HIST, S_HIST = GW - 1, SW - 1
G_SEQ0, S_SEQ0 = G_HIST + N_META + N_PROMPT, S_HIST + N_META + N_PROMPT
G_STEP, S_STEP = G_HIST + SEQ_T, S_HIST + SEQ_T
G_LEN, S_LEN = G_SEQ0 + SEQS * G_STEP, S_SEQ0 + SEQS * S_STEP

N_UP, N_DOWN, N_IN, N_OUT = FT, 2 * KT, 14, 4
A_LEN, D_LEN = 2 * KT * P, DH * P
AT_UP = (0, N_UP + N_DOWN + N_IN + N_OUT)
AT_DOWN = (N_UP, N_UP + N_DOWN + N_IN + N_OUT + N_UP)
AT_IN = N_UP + N_DOWN
AT_OUT = AT_IN + N_IN
CHUNKS = 2 * (N_UP + N_DOWN) + N_IN + N_OUT
PR_UP = (0, N_UP + N_DOWN + 2 * N_IN + 2 * N_OUT)
PR_DOWN = (N_UP, PR_UP[1] + N_UP)
PR_IN = N_UP + N_DOWN
PR_OUT = PR_IN + 2 * N_IN
PRODUCTS = 2 * (N_UP + N_DOWN) + 2 * N_IN + 2 * N_OUT

C_GAIN, C_CG, C_CS, C_GN = 0, 48, 96, 108
N_PAR = 109

MASKS = ["ident", "ones", "incl_full", "incl_seq", "strict_full", "strict_seq", "same_seq", "pair",
         "lv2", "lv4", "lv8", "lv16", "lv32", "lv64"]
LEVELS = {0: [2, 4, 8, 16, 32, 64], 1: [2, 4, 8, 16, 32, 64], 2: [2, 4, 8]}
ORDER = [2, 0, 1]


def end_of_chunk(c):
    if c < AT_IN:
        return c
    if c < AT_UP[1]:
        return PR_IN + 2 * (c - AT_IN) + 1
    return PR_UP[1] + c - AT_UP[1]


def chunk_length(c):
    return D_LEN if any(at <= c < at + N_DOWN for at in AT_DOWN) else A_LEN


def mixer_steps():
    between = {i: [] for i in range(2 * N_IN)}
    between[1] += [("gates",)]
    between[13] += [("norms",)]
    for i, t in enumerate(ORDER):
        between[13 + i] += [("decay", t), ("scores", t)]
    for i, m in enumerate([2, 4, 8, 16, 32, 64]):
        ts = [t for t in ORDER if m in LEVELS[t]]
        at = 16 + 2 * i
        between[at] += [("lv_x", t, m) for t in ts]
        between[at + 1] += [("lv_y", t, m) for t in ts]
    for n in range(2 * HEADS):
        between[n + 3].insert(0, ("sq_cols", n))
    between[23] += [("keys", 2), ("seq_read",)]
    between[24] += [("solve", 2), ("state", 2)]
    between[25] += [("attend", 2)]
    steps = []
    for i in range(2 * N_IN):
        steps += [("proj", i)] + between[i]
    steps += [("mix_y",), ("keys", 0), ("keys", 1), ("out_y",)]
    steps += [("read", 0), ("seq_state", 0, 0), ("solve", 0), ("seq_state", 0, 1), ("attend", 0), ("state", 0),
              ("seq_state", 1, 0), ("seq_state", 1, 1), ("read", 1), ("seq_state", 2, 0), ("solve", 1),
              ("seq_state", 2, 1), ("attend", 1), ("state", 1)]
    steps += [("seq_state", 3, 0), ("seq_state", 3, 1)]
    steps += [("o_norm",)] + [("o_out", t) for t in (0, 1, 2)] + [("out", m) for m in range(KT)]
    return steps


STAGE_GROUPS = {
    "decay": [("gb", "act")],
    "scores": [("qk", "dve"), ("kk", "dve"), ("vt", "dve"), ("nt", "act")],
    "lv_x": [("x", "dve")], "keys": [("kt", "dve")],
    "seq_read": [("ksT", "act"), ("kst", "dve")],
    "solve": [("nv", "dve")], "read": [("ks", "dve")], "attend": [("o", "act")], "state": [("st", "dve")],
    "o_out": [("rob", "dve")], "seq_state": [("sn", "dve")],
}


def delta_groups():
    groups, order, n = {}, [], {"dve": 0, "act": 0}
    for step in mixer_steps():
        kinds = STAGE_GROUPS.get(step[0], [])
        if step[0] == "lv_y":
            kinds = [("y", "dve"), ("yt", "dve")] if step[2] != LEVELS[step[1]][-1] else [("yt", "dve")]
        for kind, engine in kinds:
            name = (kind, *step[1:])
            of_kind = sum(other[0] == kind for other in order)
            groups[name] = (len(order), 5 + len(order) % 3, engine, n[engine], of_kind)
            order.append(name)
            n[engine] += 1
    return groups, order, n


class Signal:

    def __init__(self, sem, per_layer=0, by=1):
        self.sem, self.per, self.by = sem, per_layer, by

    def at(self, n, layer=0):
        return (layer * self.per + n + 1) * self.by


class Chain:

    def __init__(self, engine, sem):
        self.engine, self.sem, self.n = engine, sem, 0

    def step(self, ins):
        ins.then_inc(self.sem, 1)
        self.n += 1
        self.engine.wait_ge(self.sem, self.n)


def decoder_trunk(nc, io):
    ctx = ExitStack()
    with ctx:
        cursor = [(nc.sbuf_base + 63) // 64 * 64]

        def place(name, shape, dt, at):
            return nc.alloc_sbuf_tensor_at(name, shape, dt, offset=at)

        def region(nbytes):
            at = cursor[0]
            cursor[0] = (at + nbytes + 31) // 32 * 32
            return at

        def size(shape):
            return int(np.prod(shape[1:])) * 4

        def sb(name, shape, dt=F32):
            return place(name, shape, dt, region(size(shape)))

        def stack(at, *specs):
            out = []
            for name, shape, dt in specs:
                out.append(place(name, shape, dt, at))
                at += (size(shape) + 31) // 32 * 32
            return out, at

        X = sb("X", [P, KT, T])
        XH = sb("XH", [P, KT, TP], F32R)
        XL = sb("XL", [P, KT, TP], F32R)
        RAW = [sb(f"RAW{i}", [P, A_LEN]) for i in range(2)]
        WH = [sb(f"WH{i}", [P, A_LEN], F32R) for i in range(2)]
        WL = [sb(f"WL{i}", [P, A_LEN], F32R) for i in range(2)]
        W8R = sb("W8R", [P, KT * 8])
        W8H = sb("W8H", [P, KT * 8], F32R)
        W8L = sb("W8L", [P, KT * 8], F32R)
        SEQ_S = sb("SEQ_S", [P, SEQS, HEADS, P])
        PR_S = sb("PR_S", [P, HEADS, P])
        PAR_ALL = sb("PAR_ALL", [P, DEPTH, N_PAR])
        HALF_G = sb("HALF_G", [P, DEPTH, 2, KT])
        EPSC = sb("EPSC", [P, 2])
        HIST_G = sb("HIST_G", [P, DEPTH, QKV_T, SEQS, G_HIST])
        HIST_S = sb("HIST_S", [P, DEPTH, 4, SEQS, S_HIST])
        GATE_P = sb("GATE_P", [P, DEPTH, 2, HEADS])
        MK = sb("MK", [P, len(MASKS), P])
        IND = sb("IND", [P, SEQS + 1])
        RB = sb("RB", [P, T])
        SQX = [sb(f"SQX{i}", [P, TP]) for i in range(2)]
        SQY = [sb(f"SQY{i}", [P, T]) for i in range(2)]
        ACCX = sb("ACCX", [P, TP])
        ACCY = sb("ACCY", [P, TP])
        TMP = [sb(f"TMP{i}", [P, T]) for i in range(2)]
        RC = sb("RC", [P, 4, TT])
        NEW_G = sb("NEW_G", [P, QKV_T, 1 + SEQS, G_HIST])
        NEW_S = sb("NEW_S", [P, 4, 1 + SEQS, S_HIST])
        TOK = sb("TOK", [P, 16, TT, HEADS])
        B8 = sb("B8", [P, TT, 2 * HEADS])
        NEG_A = sb("NEG_A", [P, DEPTH, HEADS])
        SEQ_EL = sb("SEQ_EL", [P, HEADS, SEQS + 1])
        SSQ = sb("SSQ", [P, TT, 2 * HEADS])

        h_at = region(2 * FT * T * 4)
        (HH, HL), h_end = stack(h_at, ("HH", [P, FT, T], F32R), ("HL", [P, FT, T], F32R))
        (EXT,), at = stack(h_at, ("EXT", [P, QKV_T, G_LEN], F32))
        (NI, MI, XM0, XM1), e_end = stack(h_at, ("NI", [P, TT, HEADS, P], F32), ("MI", [P, TT, HEADS, P], F32),
                                          ("XM0", [P, HEADS, P], F32), ("XM1", [P, HEADS, P], F32))
        assert e_end <= at
        (QKV, UEXT, ZS, BY, QKM), at = stack(
            at, ("QKV", [P, QKV_T, TP], F32), ("UEXT", [P, 4, S_LEN], F32), ("ZS", [P, HEADS, T], F32),
            ("BY", [P, 4, T], F32), ("QKM", [P, TT, HEADS, P], F32))
        assert at <= h_end, (at - h_at, h_end - h_at)
        g_at = region(8 * T * 4)
        (GR0, GR1, UR0, UR1, SG0, SG1, HF0, HF1), g_end = stack(
            g_at, *[(f"{n}{i}", [P, T], F32) for n in ("GR", "UR", "SG", "HF") for i in range(2)])
        GR, UR, SG, HF = [GR0, GR1], [UR0, UR1], [SG0, SG1], [HF0, HF1]
        (VS, CV0, CV1, RB2), at = stack(g_at, ("VS", [P, TT, HEADS, P], F32), ("CV0", [P, G_LEN], F32),
                                   ("CV1", [P, G_LEN], F32), ("RB2", [P, T], F32))
        CV = [CV0, CV1]
        assert at <= g_end
        y_at = region(KT * T * 4)
        (Y,), y_end = stack(y_at, ("Y", [P, KT, T], F32))
        (DA, EGB, KST), at = stack(y_at, ("DA", [P, TT, HEADS, P], F32), ("EGB", [P, HEADS, P], F32),
                                   ("KST", [P, HEADS, P], F32))
        assert at <= y_end
        assert cursor[0] <= nc.sbuf_usable_end, (cursor[0], nc.sbuf_usable_end)
        XB = {0: XM0[:, :, :], 1: XM1[:, :, :], 2: EGB[:, :, :]}
        NVP, KTL = DA, NI

        PS = ctx.enter_context(nc.psum_tensor("PS", [P, 8, 512], F32))
        GROUPS, GROUP_ORDER, N_EVAC = delta_groups()

        def sig(name, per, by=1):
            return Signal(ctx.enter_context(nc.semaphore(name)), per, by)

        def sem(name):
            return ctx.enter_context(nc.semaphore(name))

        in_x = [sem(f"in_x{m}") for m in range(KT)]
        in_par, in_masks, in_hist, in_gate = sem("in_par"), sem("in_masks"), sem("in_hist"), sem("in_gate")
        zeroed, eps_set, gate_exp = sem("zeroed"), sem("eps_set"), sem("gate_exp")
        raw_in = [sig(f"raw_in{i}", CHUNKS // 2, 16) for i in range(2)]
        w8_in, states_in = sig("w8_in", 1, 16), sig("states_in", 1, 16)
        w8_hi, w8_lo = sig("w8_hi", 1), sig("w8_lo", 1)
        split_hi, split_lo = sig("split_hi", CHUNKS), sig("split_lo", CHUNKS)
        products = sig("products", PRODUCTS)
        x_hi, x_lo, x_sq, x_acc, x_new = (sig(n, 3 * KT) for n in ("x_hi", "x_lo", "x_sq", "x_acc", "x_new"))
        y_copied, y_sq, y_acc = (sig(n, 3 * KT) for n in ("y_copied", "y_sq", "y_acc"))
        x_cols, x_root, x_inv, x_rows, x_rb = (sig(n, 3) for n in ("x_cols", "x_root", "x_inv", "x_rows", "x_rb"))
        y_cols, y_root, y_inv, y_rows = (sig(n, 3) for n in ("y_cols", "y_root", "y_inv", "y_rows"))
        gate_scaled, up_scaled, silu_done, h_full, h_hi, h_lo = (
            sig(n, 2 * FT) for n in ("gate_scaled", "up_scaled", "silu_done", "h_full", "h_hi", "h_lo"))
        hist_set = sig("hist_set", 1)
        proj_read = sig("proj_read", 2 * N_IN)
        tap0, conv_done = sig("tap0", QKV_T + 4), sig("conv_done", QKV_T)
        act_out = sig("act_out", QKV_T + 4)
        qk_sq, qk_cols = sig("qk_sq", 2 * HEADS), sig("qk_cols", 2 * HEADS)
        mix_y, mix_hi, mix_lo = sig("mix_y", 4), sig("mix_hi", 1 + TT), sig("mix_lo", 1 + TT)
        new_hist = sig("new_hist", 2)
        small = sig("small", 3)
        to_act, to_dve = sig("to_act", 4), sig("to_dve", 4)
        gate_g = sig("gate_g", 1)
        dd_raw, dd_exp = sig("dd_raw", TT), sig("dd_exp", TT)
        pair_set = sig("pair_set", TT)
        filled = sig("filled", len(GROUP_ORDER))
        evac = {"dve": sig("evac_dve", N_EVAC["dve"]), "act": sig("evac_act", N_EVAC["act"])}
        q_decayed, kst_zero = sig("q_decayed", TT), sig("kst_zero", 1)
        seq_spread = sig("seq_spread", 2 * HEADS)
        o_inv, o_full = sig("o_inv", 1), sig("o_full", TT)
        states_out, hist_out = sig("states_out", 2, 16), sig("hist_out", 2, 16)
        out_sem = sem("out_sem")
        chain_dve, chain_act = sem("chain_dve"), sem("chain_act")

        def mask(name, width=P):
            return MK[:, MASKS.index(name), 0:width]

        def heads_of(ap):
            return ap.unsqueeze(1).to_broadcast([P, HEADS, P])

        def per_head(tok):
            return tok.unsqueeze(2).to_broadcast([P, HEADS, P])

        def incl(t):
            return mask("incl_seq" if t == C_TILE else "incl_full")

        def strict(t):
            return mask("strict_seq" if t == C_TILE else "strict_full")

        def bank(i):
            return PS[:, i, :]

        def heads_bank(name):
            return PS[:, GROUPS[name][1], :].rearrange("p (h n) -> p h n", h=HEADS)

        P8 = PS[:, 4, 0:24].rearrange("p (t c) -> p t c", t=TT)
        GCOL = PS[:, 4, 24:36].rearrange("p (t h) -> p t h", t=TT)
        GLAST = PS[:, 4, 36:48].rearrange("p (t h) -> p t h", t=TT)
        SEQ_GL = PS[:, 4, 48:84].rearrange("p (h s) -> p h s", h=HEADS)
        QK_COLS = PS[:, 4, 84:108].rearrange("p (t c) -> p t c", t=TT)
        O_COLS = PS[:, 4, 108:120].rearrange("p (t h) -> p t h", t=TT)
        Y_COLS, X_COLS = PS[:, 4, 128:131], PS[:, 4, 132:135]
        Y_ROWS, X_ROWS = PS[:, 5, 0:T], PS[:, 6, 0:T]
        (BETA, G, GC, EG, NEG_EG, KTS, EL, NK, CK, WQ, RO, T0, T1, T2, T3, T4) = (TOK[:, i, :, :] for i in range(16))

        def qT(cols):
            return QKV[:, 0:HEADS, cols]

        def kT(cols):
            return QKV[:, HEADS:2 * HEADS, cols]

        def vT(cols):
            return QKV[:, 2 * HEADS:3 * HEADS, cols]

        def tcols(t):
            return slice(t * P, (t + 1) * P)

        def gain(layer, j, after, m):
            if after and j != 1:
                return HALF_G[:, layer, j // 2, m:m + 1]
            at = C_GAIN + KT * (2 * j + after) + m
            return PAR_ALL[:, layer, at:at + 1]

        STEPS = mixer_steps()
        SEQ_NAMES = [name for name in GROUP_ORDER if name[0] == "sn"]
        LAST_SEQ_STATE = GROUPS[SEQ_NAMES[-1]][3]
        PROJ = [("qkv", i) for i in range(QKV_T)] + [("z", i) for i in range(4)] + [("b", i) for i in range(4)]
        for i in range(4):
            PROJ += [("c", i), ("h", i)]


        block = ctx.enter_context(nc.Block())

        def raw_value(layer, c):
            return raw_in[0].at(c // 2, layer)

        def tokens(f):
            return T if f < 2 * DEPTH - 1 else N_PROMPT + N_SAMPLE

        def hidden(buf, c, n):
            return buf[:, bass.ds(c, 1), 0:n].rearrange("p a t -> p (a t)") if not isinstance(c, int) else buf[:, c, 0:n]

        def seqs(ap):
            return ap.rearrange("p (s t) -> p s t", s=SEQS)

        @block.sync
        def _(sp):
            for m in range(KT):
                sp.dma_start(X[:, m, :], io["x"][:, m, :]).then_inc(in_x[m], 16)
                if m == 0:
                    sp.dma_start(PAR_ALL[:, :, :], io["par"]).then_inc(in_par, 16)
                if m == 1:
                    for slot in range(2):
                        sp.dma_start(RAW[slot][:, :], io["w_up"][0, 0, slot]).then_inc(raw_in[slot].sem, 16)
                    sp.dma_start(W8R[:, :], io["w_8"][0]).then_inc(w8_in.sem, 16)
            sp.dma_start(MK[:, :, :], io["masks"]).then_inc(in_masks, 16)
            sp.dma_start(IND[:, :], io["ind"]).then_inc(in_masks, 16)
            sp.dma_start(HIST_G[:, :, :, :, :], io["hist_g"]).then_inc(in_hist, 16)
            sp.dma_start(HIST_S[:, :, :, :, :], io["hist_s"]).then_inc(in_hist, 16)
            sp.dma_start(GATE_P[:, :, :, :], io["gate_p"].partition_broadcast(P)).then_inc(in_gate, 16)

            def run(layer, at, n, src, length, skip=0):
                with sp.Fori(skip, n // 2) as i:
                    for slot in range(2):
                        sp.wait_ge(split_lo.sem, split_lo.at(at + 2 * i + slot - 2, layer))
                        sp.dma_start(RAW[slot][:, 0:length], src(2 * i + slot)).then_inc(raw_in[slot].sem, 16)

            def row(table, c):
                return table[bass.ds(c, 1)].rearrange("a p n -> (a p) n")

            for layer in range(DEPTH):
                if layer > 0:
                    sp.wait_ge(w8_lo.sem, w8_lo.at(0, layer - 1))
                    sp.dma_start(W8R[:, :], io["w_8"][layer]).then_inc(w8_in.sem, 16)
                    sp.wait_ge(states_out.sem, states_out.at(1, layer - 1))
                sp.dma_start(SEQ_S[:, :, :, :], io["states"][layer]).then_inc(states_in.sem, 16)
                run(layer, AT_UP[0], N_UP, lambda c: row(io["w_up"][layer, 0], c), A_LEN, skip=1 if layer == 0 else 0)
                run(layer, AT_DOWN[0], N_DOWN, lambda c: row(io["w_down"][layer, 0], c), D_LEN)
                run(layer, AT_IN, N_IN, lambda c: row(io["w_in"][layer], c), A_LEN)
                run(layer, AT_OUT, N_OUT, lambda c: row(io["w_out"][layer], c), A_LEN)
                run(layer, AT_UP[1], N_UP, lambda c: row(io["w_up"][layer, 1], c), A_LEN)
                run(layer, AT_DOWN[1], N_DOWN, lambda c: row(io["w_down"][layer, 1], c), D_LEN)

        @block.gpsimd
        def _(pool):
            for buf in (XH, XL):
                pool.memset(buf[:, :, T:TP].bitcast(F32), 0.0)
            for buf in (*SQX, ACCX):
                pool.memset(buf[:, T:TP], 0.0)
            pool.memset(ACCY[:, T:TP], 0.0).then_inc(zeroed, 1)
            pool.wait_ge(in_hist, 32)
            for layer in range(DEPTH):
                pool.wait_ge(y_acc.sem, y_acc.at(KT - 1, layer))
                pool.memset(EXT[:, :, 0:G_HIST], 0.0)
                pool.memset(UEXT[:, :, 0:S_HIST], 0.0)
                pool.memset(QKV[:, :, T:TP], 0.0)
                for i in range(QKV_T):
                    pool.tensor_copy(seqs(EXT[:, i, G_SEQ0:])[:, :, 0:G_HIST], HIST_G[:, layer, i, :, :])
                for i in range(4):
                    ins = pool.tensor_copy(seqs(UEXT[:, i, S_SEQ0:])[:, :, 0:S_HIST], HIST_S[:, layer, i, :, :])
                ins.then_inc(hist_set.sem, 1)
                pool.wait_ge(x_new.sem, x_new.at(KT - 1, layer))
                pool.memset(KST[:, :, :], 0.0).then_inc(kst_zero.sem, 1)
                if layer > 0:
                    pool.wait_ge(hist_out.sem, hist_out.at(1, layer - 1))
                pool.wait_ge(proj_read.sem, proj_read.at(QKV_T - 1, layer))
                pool.tensor_copy(NEW_G[:, :, 0, :], EXT[:, :, G_SEQ0 - G_HIST:G_SEQ0])
                for i in range(QKV_T):
                    ins = pool.tensor_copy(NEW_G[:, i, 1:, :], seqs(EXT[:, i, G_SEQ0:])[:, :, SEQ_T:])
                ins.then_inc(new_hist.sem, 1)
                pool.wait_ge(new_hist.sem, new_hist.at(0, layer))
                pool.dma_start(io["new_g"][layer], NEW_G[:, :, :, :]).then_inc(hist_out.sem, 16)
                pool.wait_ge(proj_read.sem, proj_read.at(2 * N_IN - 1, layer))
                pool.tensor_copy(NEW_S[:, :, 0, :], UEXT[:, :, S_SEQ0 - S_HIST:S_SEQ0])
                for i in range(4):
                    ins = pool.tensor_copy(NEW_S[:, i, 1:, :], seqs(UEXT[:, i, S_SEQ0:])[:, :, SEQ_T:])
                ins.then_inc(new_hist.sem, 1)
                pool.wait_ge(new_hist.sem, new_hist.at(1, layer))
                pool.dma_start(io["new_s"][layer], NEW_S[:, :, :, :]).then_inc(hist_out.sem, 16)
                pool.wait_ge(evac["dve"].sem, evac["dve"].at(GROUPS[("st", 1)][3], layer))
                pool.dma_start(io["state_p"][layer], PR_S[:, :, :]).then_inc(states_out.sem, 16)
                pool.wait_ge(evac["dve"].sem, evac["dve"].at(LAST_SEQ_STATE, layer))
                pool.dma_start(io["state_s"][layer], SEQ_S[:, :, :, :]).then_inc(states_out.sem, 16)
            for m in range(KT):
                pool.wait_ge(x_new.sem, x_new.at(2 * KT + m, DEPTH - 1))
                pool.dma_start(io["y"][:, m, :], X[:, m, 0:N_PROMPT + N_SAMPLE]).then_inc(out_sem, 16)
            pool.wait_ge(out_sem, 16 * KT)
            pool.wait_ge(states_out.sem, states_out.at(1, DEPTH - 1))
            pool.wait_ge(hist_out.sem, hist_out.at(1, DEPTH - 1))

        @block.scalar
        def _(act):
            ch = Chain(act, chain_act)

            def split_high(slot, length, landed, used=None):
                act.wait_ge(raw_in[slot].sem, landed)
                if used is not None:
                    act.wait_ge(products.sem, used)
                act.activation(WH[slot][:, 0:length], RAW[slot][:, 0:length], ACT.Copy).then_inc(split_hi.sem, 1)

            def split_after(layer, c):
                nxt, at = (layer, c + 2) if c + 2 < CHUNKS else (layer + 1, c + 2 - CHUNKS)
                if nxt < DEPTH:
                    split_high(c % 2, chunk_length(at), raw_value(nxt, at), products.at(end_of_chunk(c), layer))

            def prenorm(layer, j, m):
                if (layer, j) == (0, 0):
                    act.wait_ge(in_x[m], 16)
                    if m == 0:
                        act.wait_ge(in_par, 16)
                        act.wait_ge(zeroed, 1)
                else:
                    act.wait_ge(x_new.sem, x_new.at((j - 1) * KT + m, layer))
                act.activation(XH[:, m, 0:T], X[:, m, :], ACT.Copy, scale=gain(layer, j, 0, m)).then_inc(x_hi.sem, 1)
                if m >= 2:
                    act.wait_ge(x_acc.sem, x_acc.at(j * KT + m - 2, layer))
                act.activation(SQX[m % 2][:, 0:T], X[:, m, :], ACT.Square).then_inc(x_sq.sem, 1)

            def x_norm(layer, j):
                act.wait_ge(x_cols.sem, x_cols.at(j, layer))
                act.activation(RC[:, 2, :], X_COLS, ACT.Sqrt, bias=EPSC[:, 0:1], scale=1.0 / D_MODEL).then_inc(x_root.sem, 1)

            def out_squares(layer, j, m, b, n, acc_value):
                act.wait_ge(y_copied.sem, y_copied.at(j * KT + m, layer))
                if acc_value is not None:
                    act.wait_ge(y_acc.sem, acc_value)
                act.activation(SQY[b][:, 0:n], hidden(Y, m, n), ACT.Square).then_inc(y_sq.sem, 1)

            def boundary(layer, j):
                act.wait_ge(y_cols.sem, y_cols.at(j, layer))
                act.activation(RC[:, 0, :], Y_COLS, ACT.Sqrt, bias=EPSC[:, 0:1], scale=1.0 / D_MODEL).then_inc(y_root.sem, 1)
                nxt = (layer, j + 1) if j < 2 else (layer + 1, 0)
                if nxt[0] < DEPTH:
                    for m in range(KT):
                        prenorm(*nxt, m)
                    x_norm(*nxt)

            def ffn(layer, s):
                j, n = 2 * s, tokens(2 * layer + s)

                def up_tile(c, k):
                    act.wait_ge(gate_scaled.sem, gate_scaled.at(s * FT + c, layer))
                    act.activation(SG[k][:, 0:n], GR[k][:, 0:n], ACT.Silu).then_inc(silu_done.sem, 1)
                    act.wait_ge(h_full.sem, h_full.at(s * FT + c, layer))
                    act.activation(hidden(HH, c, n), HF[k][:, 0:n], ACT.Copy).then_inc(h_hi.sem, 1)

                with act.Fori(0, N_UP // 2 - 1) as i:
                    for k in range(2):
                        split_high(k, A_LEN, raw_in[k].at(AT_UP[s] // 2 + i + 1, layer),
                                   products.at(PR_UP[s] + 2 * i + k, layer))
                        up_tile(2 * i + k, k)
                for k in range(2):
                    c = N_UP - 2 + k
                    split_after(layer, AT_UP[s] + c)
                    up_tile(c, k)
                act.preload_act_table(ACT.Sqrt)

                def squares(m, b, old):
                    out_squares(layer, j, m, b, n, y_acc.at(j * KT + m - 2, layer) if old else None)

                for b in range(2):
                    for k in range(2):
                        split_after(layer, AT_DOWN[s] + 2 * b + k)
                    squares(b, b, False)
                with act.Fori(1, KT // 2 - 1) as i:
                    for b in range(2):
                        for k in range(2):
                            split_high(k, D_LEN, raw_in[k].at(AT_DOWN[s] // 2 + 2 * i + b + 1, layer),
                                       products.at(PR_DOWN[s] + 4 * i + 2 * b + k, layer))
                        squares(2 * i + b, b, True)
                for b in range(2):
                    m = KT - 2 + b
                    for k in range(2):
                        split_after(layer, AT_DOWN[s] + 2 * m + k)
                    squares(m, b, True)

            def convolved(layer, i):
                kind, n = PROJ[i]
                if kind == "qkv":
                    cv = CV[n % 2]
                    act.wait_ge(conv_done.sem, conv_done.at(n, layer))
                    act.activation(QKV[:, n, 0:N_PROMPT], cv[:, N_META:N_META + N_PROMPT], ACT.Silu)
                    act.activation(QKV[:, n, N_PROMPT + N_SAMPLE:T], cv[:, 0:N_META], ACT.Silu)
                    ins = act.activation(seqs(QKV[:, n, N_PROMPT:N_PROMPT + N_SAMPLE]),
                                         seqs(cv[:, G_SEQ0:])[:, :, 0:SEQ_T], ACT.Silu)
                    ins.then_inc(act_out.sem, 1)
                    if n < 2 * HEADS:
                        act.wait_ge(act_out.sem, act_out.at(n, layer))
                        if n >= 2:
                            act.wait_ge(qk_cols.sem, qk_cols.at(n - 2, layer))
                        act.activation(SQX[n % 2][:, :], QKV[:, n, :], ACT.Square).then_inc(qk_sq.sem, 1)

            def projected(layer, i):
                kind, n = PROJ[i]
                if kind == "qkv":
                    act.wait_ge(proj_read.sem, proj_read.at(i, layer))
                    act.wait_ge(hist_set.sem, hist_set.at(0, layer))
                    if n >= 2:
                        act.wait_ge(act_out.sem, act_out.at(n - 2, layer))
                    act.activation(CV[n % 2][:, 0:G_LEN - 3], EXT[:, n, 0:G_LEN - 3], ACT.Copy,
                                   scale=PAR_ALL[:, layer, C_CG + n:C_CG + n + 1]).then_inc(tap0.sem, 1)
                elif kind == "z":
                    act.wait_ge(proj_read.sem, proj_read.at(i, layer))
                    act.activation(ZS[:, n, :], ZS[:, n, :], ACT.Silu).then_inc(act_out.sem, 1)
                elif kind == "h":
                    act.wait_ge(proj_read.sem, proj_read.at(i, layer))
                    if n >= 2:
                        act.wait_ge(mix_y.sem, mix_y.at(n - 2, layer))
                    else:
                        act.wait_ge(act_out.sem, act_out.at(QKV_T - 2 + n, layer))
                    act.activation(CV[n % 2][:, 0:S_LEN - 2], UEXT[:, n, 0:S_LEN - 2], ACT.Copy,
                                   scale=PAR_ALL[:, layer, C_CS + n:C_CS + n + 1]).then_inc(tap0.sem, 1)
                if i > 0:
                    convolved(layer, i - 1)
                if i % 2:
                    split_after(layer, AT_IN + i // 2)

            def evacuated(ins):
                ins.then_inc(evac["act"].sem, 1)

            def mixer(layer):
                for step in STEPS:
                    what, t = step[0], step[-1]
                    if what == "proj":
                        projected(layer, t)
                    elif what == "gates":
                        act.wait_ge(to_act.sem, to_act.at(0, layer))
                        act.activation(T0, B8[:, :, 0:HEADS], ACT.Exp, scale=-1.0)
                        ch.step(act.activation(T2, T1, ACT.Exp, scale=-1.0))
                        act.activation(T3, T2, ACT.Ln, bias=1.0).then_inc(to_dve.sem, 1)
                        act.wait_ge(small.sem, small.at(1, layer))
                        act.wait_ge(to_act.sem, to_act.at(1, layer))
                        act.activation(EG, GCOL, ACT.Exp)
                        act.activation(KTS, T2, ACT.Exp)
                        act.activation(EL, GLAST, ACT.Exp)
                        act.activation(SEQ_EL[:, :, :], SEQ_GL, ACT.Exp).then_inc(to_dve.sem, 1)
                    elif what == "norms":
                        act.wait_ge(to_act.sem, to_act.at(2, layer))
                        act.activation(NK, SSQ[:, :, HEADS:], ACT.Sqrt).then_inc(to_dve.sem, 1)
                    elif what == "decay":
                        act.wait_ge(dd_raw.sem, dd_raw.at(ORDER.index(t), layer))
                        act.activation(DA[:, t, :, :], DA[:, t, :, :], ACT.Exp).then_inc(dd_exp.sem, 1)
                        act.wait_ge(new_hist.sem, new_hist.at(0, layer))
                        evacuated(act.activation(XB[t], heads_bank(("gb", t)), ACT.Exp))
                    elif what == "scores":
                        act.wait_ge(filled.sem, filled.at(GROUPS[("nt", t)][0], layer))
                        evacuated(act.activation(NI[:, t, :, :], heads_bank(("nt", t)), ACT.Copy))
                    elif what == "seq_read":
                        act.wait_ge(filled.sem, filled.at(GROUPS[("ksT",)][0], layer))
                        act.wait_ge(kst_zero.sem, kst_zero.at(0, layer))
                        evacuated(act.activation(KST[:, :, 0:N_SAMPLE], heads_bank(("ksT",))[:, :, 0:N_SAMPLE], ACT.Copy))
                    elif what == "attend":
                        act.wait_ge(filled.sem, filled.at(GROUPS[("o", t)][0], layer))
                        act.activation(kT(tcols(t)), heads_bank(("o", t)), ACT.Copy)
                        evacuated(act.activation(vT(tcols(t)), heads_bank(("o", t)), ACT.Square))
                    elif what == "mix_y":
                        act.wait_ge(mix_y.sem, mix_y.at(3, layer))
                        act.wait_ge(products.sem, products.at(PR_IN + 2 * N_IN - 1, layer))
                        act.activation(XH[:, HEADS:KT, 0:T], BY[:, :, :], ACT.Copy).then_inc(mix_hi.sem, 1)
                    elif what == "o_norm":
                        act.wait_ge(to_act.sem, to_act.at(3, layer))
                        act.activation(T1, T0, ACT.Sqrt).then_inc(to_dve.sem, 1)
                    elif what == "o_out":
                        act.wait_ge(o_full.sem, o_full.at(t, layer))
                        cols = slice(t * P, min((t + 1) * P, T))
                        act.activation(XH[:, 0:HEADS, cols], kT(cols), ACT.Copy).then_inc(mix_hi.sem, 1)
                    elif what == "out":
                        m = t
                        out_squares(layer, 1, m, m % 2, T, y_acc.at(KT + m - 2, layer) if m >= 2 else None)
                        if m % 2:
                            split_after(layer, AT_OUT + m // 2)

            act.wait_ge(eps_set, 1)
            for slot in range(2):
                split_high(slot, A_LEN, raw_value(0, slot))
            for m in range(KT):
                prenorm(0, 0, m)
            act.wait_ge(in_gate, 16)
            act.activation(NEG_A[:, :, :], GATE_P[:, :, 0, :], ACT.Exp).then_inc(gate_exp, 1)
            x_norm(0, 0)
            for layer in range(DEPTH):
                ffn(layer, 0)
                act.wait_ge(w8_in.sem, w8_in.at(0, layer))
                if layer > 0:
                    act.wait_ge(small.sem, small.at(0, layer - 1))
                act.activation(W8H[:, :], W8R[:, :], ACT.Copy).then_inc(w8_hi.sem, 1)
                boundary(layer, 0)
                mixer(layer)
                boundary(layer, 1)
                act.wait_ge(new_hist.sem, new_hist.at(1, layer))
                ffn(layer, 1)
                boundary(layer, 2)

        @block.vector
        def _(dve):
            ch = Chain(dve, chain_dve)

            def split_low(slot, length, high):
                dve.wait_ge(split_hi.sem, high)
                dve.tensor_tensor(WL[slot][:, 0:length], RAW[slot][:, 0:length], WH[slot][:, 0:length].bitcast(F32),
                                  ALU.subtract).then_inc(split_lo.sem, 1)

            def split_after(layer, c):
                nxt, at = (layer, c + 2) if c + 2 < CHUNKS else (layer + 1, c + 2 - CHUNKS)
                if nxt < DEPTH:
                    split_low(c % 2, chunk_length(at), split_hi.at(at, nxt))

            def prenorm(layer, j, m):
                dve.wait_ge(x_hi.sem, x_hi.at(j * KT + m, layer))
                dve.scalar_tensor_tensor(XL[:, m, 0:T], X[:, m, :], gain(layer, j, 0, m), XH[:, m, 0:T].bitcast(F32),
                                         ALU.mult, ALU.subtract).then_inc(x_lo.sem, 1)
                dve.wait_ge(x_sq.sem, x_sq.at(j * KT + m, layer))
                if m == 0:
                    ins = dve.tensor_copy(ACCX[:, 0:T], SQX[0][:, 0:T])
                else:
                    dve.wait_ge(x_acc.sem, x_acc.at(j * KT + m - 1, layer))
                    ins = dve.tensor_tensor(ACCX[:, 0:T], ACCX[:, 0:T], SQX[m % 2][:, 0:T], ALU.add)
                ins.then_inc(x_acc.sem, 1)

            def x_norm(layer, j):
                dve.wait_ge(x_root.sem, x_root.at(j, layer))
                dve.reciprocal(RC[:, 3, :], RC[:, 2, :]).then_inc(x_inv.sem, 1)
                dve.wait_ge(x_rows.sem, x_rows.at(j, layer))
                dve.tensor_copy(RB[:, :], X_ROWS).then_inc(x_rb.sem, 1)
                dve.wait_ge(x_rb.sem, x_rb.at(j, layer))

            def out_tile(layer, j, m, b, n, done, ps, before):
                dve.wait_ge(products.sem, done)
                dve.tensor_copy(hidden(Y, m, n), ps[:, 0:n]).then_inc(y_copied.sem, 1)
                dve.wait_ge(y_sq.sem, y_sq.at(j * KT + m, layer))
                if before is None:
                    ins = dve.tensor_copy(ACCY[:, 0:n], SQY[b][:, 0:n])
                else:
                    dve.wait_ge(y_acc.sem, before)
                    ins = dve.tensor_tensor(ACCY[:, 0:n], ACCY[:, 0:n], SQY[b][:, 0:n], ALU.add)
                ins.then_inc(y_acc.sem, 1)

            def boundary(layer, j):
                n = tokens(2 * layer + 1) if j == 2 else T
                nxt = (layer, j + 1) if j < 2 else (layer + 1, 0)
                dve.wait_ge(y_root.sem, y_root.at(j, layer))
                dve.reciprocal(RC[:, 1, :], RC[:, 0, :]).then_inc(y_inv.sem, 1)
                dve.wait_ge(y_rows.sem, y_rows.at(j, layer))
                for m in range(KT):
                    tmp = TMP[m % 2][:, 0:n]
                    if m >= 2:
                        dve.wait_ge(x_new.sem, x_new.at(j * KT + m - 2, layer))
                    ch.step(dve.scalar_tensor_tensor(tmp, Y[:, m, 0:n], gain(layer, j, 1, m), Y_ROWS[:, 0:n],
                                                     ALU.mult, ALU.mult))
                    dve.tensor_tensor(X[:, m, 0:n], X[:, m, 0:n], tmp, ALU.add).then_inc(x_new.sem, 1)
                    if m > 0 and nxt[0] < DEPTH:
                        prenorm(*nxt, m - 1)
                if nxt[0] < DEPTH:
                    prenorm(*nxt, KT - 1)
                    x_norm(*nxt)

            def ffn(layer, s):
                j, n = 2 * s, tokens(2 * layer + s)

                def up_tile(c, k, split):
                    dve.wait_ge(products.sem, products.at(PR_UP[s] + c, layer))
                    dve.tensor_tensor(GR[k][:, 0:n], PS[:, 2 * k, 0:n], RB[:, 0:n], ALU.mult).then_inc(gate_scaled.sem, 1)
                    dve.tensor_tensor(UR[k][:, 0:n], PS[:, 2 * k + 1, 0:n], RB[:, 0:n], ALU.mult).then_inc(up_scaled.sem, 1)
                    split()
                    dve.wait_ge(silu_done.sem, silu_done.at(s * FT + c, layer))
                    dve.wait_ge(up_scaled.sem, up_scaled.at(s * FT + c, layer))
                    dve.tensor_tensor(HF[k][:, 0:n], SG[k][:, 0:n], UR[k][:, 0:n], ALU.mult).then_inc(h_full.sem, 1)
                    dve.wait_ge(h_hi.sem, h_hi.at(s * FT + c, layer))
                    dve.tensor_tensor(hidden(HL, c, n), HF[k][:, 0:n], hidden(HH, c, n).bitcast(F32),
                                      ALU.subtract).then_inc(h_lo.sem, 1)

                with dve.Fori(0, N_UP // 2 - 1) as i:
                    for k in range(2):
                        up_tile(2 * i + k, k, lambda: split_low(k, A_LEN, split_hi.at(AT_UP[s] + 2 * i + k + 2, layer)))
                for k in range(2):
                    c = N_UP - 2 + k
                    up_tile(c, k, lambda: split_after(layer, AT_UP[s] + c))

                def out(m, b, old):
                    out_tile(layer, j, m, b, n, products.at(PR_DOWN[s] + 2 * m + 1, layer), PS[:, 2 * b, :],
                             y_acc.at(j * KT + m - 1, layer) if old else None)

                for b in range(2):
                    for k in range(2):
                        split_after(layer, AT_DOWN[s] + 2 * b + k)
                    out(b, b, b > 0)
                with dve.Fori(1, KT // 2 - 1) as i:
                    for b in range(2):
                        for k in range(2):
                            split_low(k, D_LEN, split_hi.at(AT_DOWN[s] + 4 * i + 2 * b + k + 2, layer))
                        out(2 * i + b, b, True)
                for b in range(2):
                    m = KT - 2 + b
                    if b == 0:
                        for k in range(2):
                            split_after(layer, AT_DOWN[s] + 2 * m + k)
                    out(m, b, True)
                    if b == 1:
                        for k in range(2):
                            split_after(layer, AT_DOWN[s] + 2 * m + k)

            def convolved(layer, i):
                kind, n = PROJ[i]
                if kind not in ("qkv", "h"):
                    return
                at, taps, steps, src, length = ((C_CG, GW, QKV_T, EXT, G_LEN) if kind == "qkv"
                                                else (C_CS, SW, 4, UEXT, S_LEN))
                k = n % 2
                cv = CV[k][:, 0:length - taps + 1]
                dve.wait_ge(tap0.sem, tap0.at(n + (QKV_T if kind == "h" else 0), layer))
                for tap in range(1, taps):
                    col = at + tap * steps + n
                    ins = dve.scalar_tensor_tensor(cv, src[:, n, tap:tap + length - taps + 1],
                                                   PAR_ALL[:, layer, col:col + 1], cv, ALU.mult, ALU.add)
                    if tap < taps - 1 or kind == "h":
                        ch.step(ins)
                    else:
                        ins.then_inc(conv_done.sem, 1)
                if kind == "h":
                    by = BY[:, n, :]
                    dve.tensor_tensor(by[:, 0:N_PROMPT], by[:, 0:N_PROMPT], CV[k][:, N_META:N_META + N_PROMPT], ALU.mult)
                    dve.tensor_tensor(by[:, N_PROMPT + N_SAMPLE:T], by[:, N_PROMPT + N_SAMPLE:T], CV[k][:, 0:N_META],
                                      ALU.mult)
                    dve.tensor_tensor(seqs(by[:, N_PROMPT:N_PROMPT + N_SAMPLE]), seqs(by[:, N_PROMPT:N_PROMPT + N_SAMPLE]),
                                      seqs(CV[k][:, S_SEQ0:S_SEQ0 + SEQS * S_STEP])[:, :, 0:SEQ_T],
                                      ALU.mult).then_inc(mix_y.sem, 1)

            def spread(dst, hist, seq0, step, ps, by):
                dve.tensor_tensor(dst[:, hist:hist + N_META], ps[:, N_PROMPT + N_SAMPLE:T],
                                  by[:, N_PROMPT + N_SAMPLE:T], ALU.mult)
                dve.tensor_tensor(dst[:, hist + N_META:seq0], ps[:, 0:N_PROMPT], by[:, 0:N_PROMPT], ALU.mult)
                return dve.tensor_tensor(seqs(dst[:, seq0:])[:, :, hist:], seqs(ps[:, N_PROMPT:N_PROMPT + N_SAMPLE]),
                                         seqs(by[:, N_PROMPT:N_PROMPT + N_SAMPLE]), ALU.mult)

            def projected(layer, i):
                kind, n = PROJ[i]
                ps = PS[:, i % 4, :]
                if i == 0:
                    dve.wait_ge(hist_set.sem, hist_set.at(0, layer))
                    ch.step(dve.tensor_tensor(RB2[:, :], RB[:, :], RB[:, :], ALU.mult))
                dve.wait_ge(products.sem, products.at(PR_IN + i, layer))
                if kind == "qkv":
                    ins = spread(EXT[:, n, :], G_HIST, G_SEQ0, G_STEP, ps, RB)
                elif kind == "z":
                    ins = dve.tensor_tensor(ZS[:, n, :], ps[:, 0:T], RB[:, :], ALU.mult)
                elif kind == "b":
                    ins = dve.tensor_tensor(BY[:, n, :], ps[:, 0:T], RB[:, :], ALU.mult)
                elif kind == "c":
                    ins = dve.tensor_tensor(TMP[n % 2][:, :], ps[:, 0:T], RB2[:, :], ALU.mult)
                else:
                    dve.wait_ge(proj_read.sem, proj_read.at(i - 1, layer))
                    ins = spread(UEXT[:, n, :], S_HIST, S_SEQ0, S_STEP, ps, TMP[n % 2])
                ins.then_inc(proj_read.sem, 1)
                if i > 0:
                    convolved(layer, i - 1)
                if i % 2:
                    split_after(layer, AT_IN + i // 2)

            def group(name, layer):
                dve.wait_ge(filled.sem, filled.at(GROUPS[name][0], layer))
                return heads_bank(name)

            def evacuated(ins):
                ins.then_inc(evac["dve"].sem, 1)

            def act_group(name, layer):
                dve.wait_ge(evac["act"].sem, evac["act"].at(GROUPS[name][3], layer))

            def mixer(layer):
                for step in STEPS:
                    what, t = step[0], step[-1]
                    if what == "proj":
                        projected(layer, t)
                    elif what == "gates":
                        dve.wait_ge(small.sem, small.at(0, layer))
                        ch.step(dve.tensor_tensor(B8[:, :, :], P8, RC[:, 3, :].unsqueeze(2).to_broadcast([P, TT, 2 * HEADS]),
                                                  ALU.mult))
                        dt_bias = GATE_P[:, layer, 1, :].unsqueeze(1).to_broadcast([P, TT, HEADS])
                        ch.step(dve.tensor_tensor(T4, B8[:, :, HEADS:], dt_bias, ALU.add))
                        dve.scalar_tensor_tensor(T1, T4, -1.0, T4, ALU.mult, ALU.max).then_inc(to_act.sem, 1)
                        dve.wait_ge(to_dve.sem, to_dve.at(0, layer))
                        ch.step(dve.tensor_scalar(T0, T0, 1.0, None, ALU.add))
                        dve.reciprocal(BETA, T0)
                        ch.step(dve.scalar_tensor_tensor(T3, T4, 0.0, T3, ALU.max, ALU.add))
                        neg_a = NEG_A[:, layer, :].unsqueeze(1).to_broadcast([P, TT, HEADS])
                        dve.scalar_tensor_tensor(G, T3, -1.0, neg_a, ALU.mult, ALU.mult).then_inc(gate_g.sem, 1)
                        dve.wait_ge(small.sem, small.at(1, layer))
                        ch.step(dve.tensor_copy(GC, GCOL))
                        dve.tensor_tensor(T2, GLAST, GC, ALU.subtract).then_inc(to_act.sem, 1)
                        dve.wait_ge(to_dve.sem, to_dve.at(1, layer))
                        ch.step(dve.tensor_scalar(NEG_EG, EG, -1.0, None, ALU.mult))
                    elif what == "norms":
                        dve.wait_ge(qk_cols.sem, qk_cols.at(2 * HEADS - 1, layer))
                        ch.step(dve.tensor_scalar(SSQ[:, :, :], QK_COLS, EPS, None, ALU.add))
                        dve.reciprocal(T0, SSQ[:, :, HEADS:]).then_inc(to_act.sem, 1)
                        dve.wait_ge(to_act.sem, to_act.at(2, layer))
                        dve.tensor_tensor(CK, T0, BETA, ALU.mult)
                        ch.step(dve.tensor_scalar(WQ, SSQ[:, :, 0:HEADS], EPS * P, None, ALU.mult))
                        dve.wait_ge(to_dve.sem, to_dve.at(2, layer))
                    elif what == "decay":
                        gb = group(("gb", t), layer)
                        for h in range(HEADS):
                            ins = dve.tensor_scalar(DA[:, t, h, :], gb[:, h, :], GC[:, t, h:h + 1], 0.0, ALU.subtract, ALU.min)
                        ins.then_inc(dd_raw.sem, 1)
                    elif what == "scores":
                        dve.wait_ge(dd_exp.sem, dd_exp.at(ORDER.index(t), layer))
                        ins = dve.tensor_tensor(QKM[:, t, :, :], group(("qk", t), layer), DA[:, t, :, :], ALU.mult)
                        evacuated(ins)
                        dve.wait_ge(evac["dve"].sem, evac["dve"].at(GROUPS[("qk", t)][3], layer))
                        dve.tensor_tensor(QKM[:, t, :, :], QKM[:, t, :, :], heads_of(incl(t)), ALU.mult)
                        kk = group(("kk", t), layer)
                        for h in range(HEADS):
                            ins = dve.scalar_tensor_tensor(DA[:, t, h, :], kk[:, h, :], CK[:, t, h:h + 1], DA[:, t, h, :],
                                                           ALU.mult, ALU.mult)
                        evacuated(ins)
                        dve.wait_ge(evac["dve"].sem, evac["dve"].at(GROUPS[("kk", t)][3], layer))
                        ch.step(dve.tensor_tensor(DA[:, t, :, :], DA[:, t, :, :], heads_of(strict(t)), ALU.mult))
                        if t == ORDER[0]:
                            dve.wait_ge(new_hist.sem, new_hist.at(0, layer))
                            dve.wait_ge(conv_done.sem, conv_done.at(QKV_T - 1, layer))
                        ch.step(dve.tensor_tensor(MI[:, t, :, :], DA[:, t, :, :], heads_of(mask("pair")), ALU.mult))
                        dve.tensor_tensor(MI[:, t, :, :], heads_of(mask("ident")), MI[:, t, :, :],
                                          ALU.subtract).then_inc(pair_set.sem, 1)
                        evacuated(dve.tensor_tensor(VS[:, t, :, :], group(("vt", t), layer), per_head(NK[:, t, :]), ALU.mult))
                        act_group(("gb", t), layer)
                        dve.tensor_tensor(qT(tcols(t)), qT(tcols(t)), XB[t], ALU.mult).then_inc(q_decayed.sem, 1)
                        dve.wait_ge(q_decayed.sem, q_decayed.at(ORDER.index(t), layer))
                    elif what == "lv_x":
                        _, t, m = step
                        evacuated(dve.tensor_tensor(XB[t], group(("x", t, m), layer), heads_of(mask(f"lv{m}")), ALU.mult))
                    elif what == "lv_y":
                        _, t, m = step
                        if ("y", t, m) in GROUPS:
                            evacuated(dve.tensor_tensor(NI[:, t, :, :], NI[:, t, :, :], group(("y", t, m), layer), ALU.subtract))
                        evacuated(dve.tensor_tensor(MI[:, t, :, :], MI[:, t, :, :], group(("yt", t, m), layer), ALU.subtract))
                    elif what == "keys":
                        evacuated(dve.tensor_tensor(KTL[:, t, :, :], group(("kt", t), layer), per_head(KTS[:, t, :]), ALU.mult))
                    elif what in ("seq_read", "read"):
                        name, t = (("kst",), C_TILE) if what == "seq_read" else (("ks", t), t)
                        ks = group(name, layer)
                        for h in range(HEADS):
                            ins = dve.scalar_tensor_tensor(VS[:, t, h, :], ks[:, h, :], NEG_EG[:, t, h:h + 1], VS[:, t, h, :],
                                                           ALU.mult, ALU.add)
                        evacuated(ins)
                    elif what == "solve":
                        evacuated(dve.tensor_tensor(NVP[:, t, :, :], group(("nv", t), layer), per_head(CK[:, t, :]), ALU.mult))
                    elif what == "state":
                        st = group(("st", t), layer)
                        if t == C_TILE:
                            if layer > 0:
                                dve.wait_ge(states_out.sem, states_out.at(1, layer - 1))
                            ins = dve.tensor_copy(PR_S[:, :, :], st)
                        else:
                            for h in range(HEADS):
                                ins = dve.scalar_tensor_tensor(PR_S[:, h, :], PR_S[:, h, :], EL[:, t, h:h + 1], st[:, h, :],
                                                               ALU.mult, ALU.add)
                        evacuated(ins)
                    elif what == "mix_y":
                        convolved(layer, 2 * N_IN - 1)
                        dve.wait_ge(mix_hi.sem, mix_hi.at(0, layer))
                        dve.tensor_tensor(XL[:, HEADS:KT, 0:T], BY[:, :, :], XH[:, HEADS:KT, 0:T].bitcast(F32),
                                          ALU.subtract).then_inc(mix_lo.sem, 1)
                    elif what == "seq_state":
                        _, h, half = step
                        k = GROUPS[("sn", h, half)][4]
                        buf = [XM0, XM1][k % 2]
                        per_seq = NVP[0:N_SAMPLE, C_TILE, h, :].unsqueeze(1).to_broadcast([N_SAMPLE, 4, P])
                        which = IND[0:N_SAMPLE, 4 * half:4 * half + 4].unsqueeze(2).to_broadcast([N_SAMPLE, 4, P])
                        if k >= 2:
                            dve.wait_ge(filled.sem, filled.at(GROUPS[SEQ_NAMES[k - 2]][0], layer))
                        dve.tensor_tensor(buf[0:N_SAMPLE, :, :], per_seq, which, ALU.mult).then_inc(seq_spread.sem, 1)
                        sn = group(("sn", h, half), layer)
                        for q in range(4):
                            s = 4 * half + q
                            ins = dve.scalar_tensor_tensor(SEQ_S[:, s, h, :], SEQ_S[:, s, h, :], SEQ_EL[:, h, s:s + 1],
                                                           sn[:, q, :], ALU.mult, ALU.add)
                        evacuated(ins)
                    elif what == "o_norm":
                        dve.wait_ge(small.sem, small.at(2, layer))
                        dve.scalar_tensor_tensor(T0, O_COLS, 1.0 / P, WQ, ALU.mult, ALU.add).then_inc(to_act.sem, 1)
                        dve.wait_ge(to_dve.sem, to_dve.at(3, layer))
                        dve.reciprocal(RO, T1).then_inc(o_inv.sem, 1)
                    elif what == "o_out":
                        cols = slice(t * P, min((t + 1) * P, T))
                        n = cols.stop - cols.start
                        act_group(("o", t), layer)
                        rob = group(("rob", t), layer)
                        ins = dve.scalar_tensor_tensor(kT(cols), kT(cols), PAR_ALL[:, layer, C_GN:C_GN + 1], rob[:, :, 0:n],
                                                       ALU.mult, ALU.mult)
                        evacuated(ins)
                        dve.wait_ge(evac["dve"].sem, evac["dve"].at(GROUPS[("rob", t)][3], layer))
                        dve.wait_ge(act_out.sem, act_out.at(QKV_T + 3, layer))
                        dve.tensor_tensor(kT(cols), kT(cols), ZS[:, :, cols], ALU.mult).then_inc(o_full.sem, 1)
                        dve.wait_ge(mix_hi.sem, mix_hi.at(1 + t, layer))
                        dve.tensor_tensor(XL[:, 0:HEADS, cols], kT(cols), XH[:, 0:HEADS, cols].bitcast(F32),
                                          ALU.subtract).then_inc(mix_lo.sem, 1)
                    elif what == "out":
                        m = t
                        out_tile(layer, 1, m, m % 2, T, products.at(PR_OUT + m, layer), PS[:, m % 4, :],
                                 y_acc.at(KT + m - 1, layer) if m else None)
                        if m % 2:
                            split_after(layer, AT_OUT + m // 2)

            dve.memset(EPSC[:, :], EPS).then_inc(eps_set, 1)
            dve.wait_ge(in_par, 16)
            for layer in range(DEPTH):
                for s in range(2):
                    at = C_GAIN + KT * (4 * s + 1)
                    ch.step(dve.tensor_scalar(HALF_G[:, layer, s, :], PAR_ALL[:, layer, at:at + KT], 0.5, None, ALU.mult))
            for slot in range(2):
                split_low(slot, A_LEN, split_hi.at(slot))
            for m in range(KT):
                if m == 0:
                    dve.wait_ge(zeroed, 1)
                prenorm(0, 0, m)
            x_norm(0, 0)
            dve.wait_ge(gate_exp, 1)
            for layer in range(DEPTH):
                ffn(layer, 0)
                dve.wait_ge(w8_hi.sem, w8_hi.at(0, layer))
                dve.tensor_tensor(W8L[:, :], W8R[:, :], W8H[:, :].bitcast(F32), ALU.subtract).then_inc(w8_lo.sem, 1)
                boundary(layer, 0)
                mixer(layer)
                boundary(layer, 1)
                dve.wait_ge(new_hist.sem, new_hist.at(1, layer))
                ffn(layer, 1)
                boundary(layer, 2)

        @block.tensor
        def _(pe):
            def three(out, wh, wl, xh, xl, first, last):
                pe.matmul(out, wh, xh, start=first, stop=False)
                pe.matmul(out, wh, xl, start=False, stop=False)
                return pe.matmul(out, wl, xh, start=False, stop=last)

            def block_of(slot, at):
                return WH[slot][:, at * P:(at + 1) * P], WL[slot][:, at * P:(at + 1) * P]

            def x_tile(kt, n):
                return XH[:, kt, 0:n], XL[:, kt, 0:n]

            def columns(acc, out, ready):
                pe.wait_ge(ready[0], ready[1])
                for t in range(TT):
                    ins = pe.matmul(out[:, t:t + 1], acc[:, tcols(t)], mask("ones", 1), start=True, stop=True)
                return ins

            def rows(col, out):
                for t in range(TT):
                    n = min(P, T - t * P)
                    ins = pe.matmul(out[:, t * P:t * P + n], col[:, t:t + 1].to_broadcast([P, P]), mask("ident", n),
                                    start=True, stop=True)
                return ins

            def entry(layer, j, at, n, first_product):
                for slot in range(2):
                    pe.wait_ge(split_lo.sem, split_lo.at(at + slot, layer))
                early = 5

                def part(slot, kt):
                    for half in range(2):
                        ins = three(PS[:, 2 * slot + half, 0:n], *block_of(slot, half * KT + kt), *x_tile(kt, n),
                                    kt == 0, kt == KT - 1)
                        if kt == KT - 1 and (half == 1 or first_product):
                            ins.then_inc(products.sem, 1)

                def ready(kt):
                    pe.wait_ge(x_lo.sem, x_lo.at(j * KT + kt, layer))

                for kt in range(early):
                    ready(kt)
                    part(0, kt)
                    part(1, kt)
                for kt in range(early, KT):
                    ready(kt)
                    part(0, kt)
                columns(ACCX, X_COLS, (x_acc.sem, x_acc.at(j * KT + KT - 1, layer))).then_inc(x_cols.sem, 1)
                for kt in range(early, KT):
                    part(1, kt)
                pe.wait_ge(x_inv.sem, x_inv.at(j, layer))
                rows(RC[:, 3, :], X_ROWS).then_inc(x_rows.sem, 1)

            def ffn(layer, s):
                j, n = 2 * s, tokens(2 * layer + s)
                entry(layer, j, AT_UP[s], n, False)

                def up_chunk(i, k):
                    c = 2 * i + k
                    pe.wait_ge(split_lo.sem, split_lo.at(AT_UP[s] + c, layer))
                    pe.wait_ge(up_scaled.sem, up_scaled.at(s * FT + c - 2, layer))
                    for half in range(2):
                        for kt in range(KT):
                            ins = three(PS[:, 2 * k + half, 0:n], *block_of(k, half * KT + kt), *x_tile(kt, n),
                                        kt == 0, kt == KT - 1)
                    ins.then_inc(products.sem, 1)

                with pe.Fori(1, N_UP // 2) as i:
                    for k in range(2):
                        up_chunk(i, k)

                def down_tile(m, b, first=False, old=True):
                    for half in range(2):
                        pe.wait_ge(split_lo.sem, split_lo.at(AT_DOWN[s] + 2 * m + half, layer))
                        if half == 0 and old:
                            pe.wait_ge(y_copied.sem, y_copied.at(j * KT + m - 2, layer))
                        if half == 0 and not old:
                            pe.wait_ge(gate_scaled.sem, gate_scaled.at(s * FT + FT - 2 + b, layer))
                        for q in range(DH):
                            f = half * DH + q
                            if first:
                                pe.wait_ge(h_lo.sem, h_lo.at(s * FT + f, layer))
                            ins = three(PS[:, 2 * b, 0:n], *block_of(half, q), HH[:, f, 0:n], HL[:, f, 0:n],
                                        f == 0, f == FT - 1)
                        ins.then_inc(products.sem, 1)

                down_tile(0, 0, first=True, old=False)
                down_tile(1, 1, old=False)
                with pe.Fori(1, KT // 2) as i:
                    for b in range(2):
                        down_tile(2 * i + b, b)

            def out_norm(layer, j):
                columns(ACCY, Y_COLS, (y_acc.sem, y_acc.at(j * KT + KT - 1, layer))).then_inc(y_cols.sem, 1)
                pe.wait_ge(y_inv.sem, y_inv.at(j, layer))
                rows(RC[:, 1, :], Y_ROWS).then_inc(y_rows.sem, 1)

            def evacuated(name, layer):
                _, _, engine, count, _ = GROUPS[name]
                pe.wait_ge(evac[engine].sem, evac[engine].at(count, layer))

            def group(name, layer):
                index = GROUPS[name][0]
                if index >= 3:
                    evacuated(GROUP_ORDER[index - 3], layer)
                return heads_bank(name)

            def per_head_products(name, layer, lhsT, rhs, transpose=False):
                out = group(name, layer)
                for h in range(HEADS):
                    if transpose:
                        ins = pe.transpose(out[:, h, :], lhsT(h), mask("ident"))
                    else:
                        ins = pe.matmul(out[:, h, :], lhsT(h), rhs(h), start=True, stop=True)
                ins.then_inc(filled.sem, 1)

            def mixer(layer):
                for step in STEPS:
                    what, t = step[0], step[-1]
                    if what == "proj":
                        i = t
                        if i == 0:
                            entry(layer, 1, AT_IN, T, True)
                        if i < 4:
                            continue
                        pe.wait_ge(proj_read.sem, proj_read.at(i - 4, layer))
                        slot = (i // 2) % 2
                        pe.wait_ge(split_lo.sem, split_lo.at(AT_IN + i // 2, layer))
                        for kt in range(KT):
                            ins = three(PS[:, i % 4, 0:T], *block_of(slot, (i % 2) * KT + kt), *x_tile(kt, T),
                                        kt == 0, kt == KT - 1)
                        ins.then_inc(products.sem, 1)
                    elif what == "sq_cols":
                        pe.wait_ge(qk_sq.sem, qk_sq.at(t, layer))
                        if t == 0:
                            pe.wait_ge(to_dve.sem, to_dve.at(1, layer))
                        for q in range(TT):
                            ins = pe.matmul(QK_COLS[:, q, t:t + 1], SQX[t % 2][:, tcols(q)], mask("ones", 1),
                                            start=True, stop=True)
                        ins.then_inc(qk_cols.sem, 1)
                    elif what == "gates":
                        pe.wait_ge(w8_lo.sem, w8_lo.at(0, layer))
                        for q in range(TT):
                            for kt in range(KT):
                                xh, xl = XH[:, kt, tcols(q)], XL[:, kt, tcols(q)]
                                wh, wl = W8H[:, 8 * kt:8 * kt + 8], W8L[:, 8 * kt:8 * kt + 8]
                                ins = three(P8[:, q, :], xh, xl, wh, wl, kt == 0, kt == KT - 1)
                        ins.then_inc(small.sem, 1)
                        pe.wait_ge(gate_g.sem, gate_g.at(0, layer))
                        for q in range(TT):
                            pe.matmul(GCOL[:, q, :], incl(q), G[:, q, :], start=True, stop=True)
                            pe.matmul(GLAST[:, q, :], mask("same_seq" if q == C_TILE else "ones"), G[:, q, :],
                                      start=True, stop=True)
                        for h in range(HEADS):
                            ins = pe.matmul(SEQ_GL[:, h, :], G[:, C_TILE, h:h + 1].to_broadcast([P, P]), IND[:, :],
                                            start=True, stop=True)
                        ins.then_inc(small.sem, 1)
                    elif what == "decay":
                        per_head_products(("gb", t), layer, lambda h: G[:, t, h:h + 1].to_broadcast([P, P]),
                                          lambda h: incl(t))
                    elif what == "scores":
                        pe.wait_ge(act_out.sem, act_out.at(QKV_T - 1, layer))
                        per_head_products(("qk", t), layer, lambda h: kT(tcols(t))[:, h, :], lambda h: qT(tcols(t))[:, h, :])
                        per_head_products(("kk", t), layer, lambda h: kT(tcols(t))[:, h, :], lambda h: kT(tcols(t))[:, h, :])
                        per_head_products(("vt", t), layer, lambda h: vT(tcols(t))[:, h, :], None, transpose=True)
                        pe.wait_ge(pair_set.sem, pair_set.at(ORDER.index(t), layer))
                        per_head_products(("nt", t), layer, lambda h: MI[:, t, h, :], None, transpose=True)
                    elif what == "lv_x":
                        _, t, m = step
                        evacuated(("nt", t) if m == 2 else ("y", t, m // 2), layer)
                        if m == 2:
                            pe.wait_ge(q_decayed.sem, q_decayed.at(ORDER.index(t), layer))
                        per_head_products(("x", t, m), layer, lambda h: DA[:, t, h, :], lambda h: NI[:, t, h, :])
                    elif what == "lv_y":
                        _, t, m = step
                        evacuated(("x", t, m), layer)
                        if m > 2:
                            evacuated(("yt", t, m // 2), layer)
                        if ("y", t, m) in GROUPS:
                            per_head_products(("y", t, m), layer, lambda h: MI[:, t, h, :], lambda h: XB[t][:, h, :])
                        per_head_products(("yt", t, m), layer, lambda h: XB[t][:, h, :], lambda h: MI[:, t, h, :])
                    elif what == "keys":
                        per_head_products(("kt", t), layer, lambda h: kT(tcols(t))[:, h, :], None, transpose=True)
                    elif what == "seq_read":
                        pe.wait_ge(states_in.sem, states_in.at(0, layer))
                        out = group(("ksT",), layer)
                        for h in range(HEADS):
                            for s in range(SEQS):
                                cols = slice(N_PROMPT + s * SEQ_T, N_PROMPT + (s + 1) * SEQ_T)
                                ins = pe.matmul(out[:, h, s * SEQ_T:(s + 1) * SEQ_T], SEQ_S[:, s, h, :], kT(cols)[:, h, :],
                                                start=True, stop=True)
                        ins.then_inc(filled.sem, 1)
                        evacuated(("ksT",), layer)
                        per_head_products(("kst",), layer, lambda h: KST[:, h, :], None, transpose=True)
                    elif what == "read":
                        evacuated(("st", C_TILE if t == 0 else 0), layer)
                        per_head_products(("ks", t), layer, lambda h: kT(tcols(t))[:, h, :], lambda h: PR_S[:, h, :])
                    elif what == "solve":
                        evacuated(("kst",) if t == C_TILE else ("ks", t), layer)
                        evacuated(("yt", t, LEVELS[t][-1]), layer)
                        per_head_products(("nv", t), layer, lambda h: MI[:, t, h, :], lambda h: VS[:, t, h, :])
                    elif what == "state":
                        evacuated(("nv", t), layer)
                        evacuated(("kt", t), layer)
                        part = slice(META_AT, META_AT + N_META) if t == C_TILE else slice(0, P)
                        per_head_products(("st", t), layer, lambda h: KTL[part, t, h, :], lambda h: NVP[part, t, h, :])
                    elif what == "attend":
                        evacuated(("nv", t), layer)
                        out = group(("o", t), layer)
                        for h in range(HEADS):
                            if t != C_TILE:
                                pe.matmul(out[:, h, :], NVP[:, t, h, :], QKM[:, t, h, :], start=True, stop=False)
                                ins = pe.matmul(out[:, h, :], PR_S[:, h, :], qT(tcols(t))[:, h, :], start=False, stop=True)
                                continue
                            for s in range(SEQS):
                                cols = slice(N_PROMPT + s * SEQ_T, N_PROMPT + (s + 1) * SEQ_T)
                                pe.matmul(out[:, h, s * SEQ_T:(s + 1) * SEQ_T], SEQ_S[:, s, h, :], qT(cols)[:, h, :],
                                          start=(s == 0), stop=False)
                            pe.matmul(out[:, h, 0:N_SAMPLE], NVP[:, t, h, :], QKM[:, t, h, 0:N_SAMPLE],
                                      start=False, stop=True)
                            ins = pe.matmul(out[:, h, N_SAMPLE:], NVP[:, t, h, :], QKM[:, t, h, N_SAMPLE:],
                                            start=True, stop=True)
                        ins.then_inc(filled.sem, 1)
                    elif what == "seq_state":
                        _, h, half = step
                        k = GROUPS[("sn", h, half)][4]
                        pe.wait_ge(seq_spread.sem, seq_spread.at(k, layer))
                        out = group(("sn", h, half), layer)
                        pe.matmul(out, KTL[0:N_SAMPLE, C_TILE, h, :], [XM0, XM1][k % 2][0:N_SAMPLE, :, :],
                                  start=True, stop=True).then_inc(filled.sem, 1)
                    elif what == "o_norm":
                        evacuated(("o", 1), layer)
                        for q in range(TT):
                            for h in range(HEADS):
                                ins = pe.matmul(O_COLS[:, q, h:h + 1], vT(tcols(q))[:, h, :], mask("ones", 1),
                                                start=True, stop=True)
                        ins.then_inc(small.sem, 1)
                    elif what == "o_out":
                        pe.wait_ge(o_inv.sem, o_inv.at(0, layer))
                        per_head_products(("rob", t), layer, lambda h: RO[:, t, h:h + 1].to_broadcast([P, P]),
                                          lambda h: mask("ident"))
                    elif what == "out_y":
                        pe.wait_ge(mix_lo.sem, mix_lo.at(0, layer))
                        for m in range(4):
                            pe.wait_ge(split_lo.sem, split_lo.at(AT_OUT + m // 2, layer))
                            pe.wait_ge(proj_read.sem, proj_read.at(2 * N_IN - 4 + m, layer))
                            for kt in range(HEADS, KT):
                                three(PS[:, m, 0:T], *block_of(m // 2, (m % 2) * KT + kt), *x_tile(kt, T),
                                      kt == HEADS, False)
                    elif what == "out":
                        m = t
                        slot = (m // 2) % 2
                        if m == 0:
                            pe.wait_ge(mix_lo.sem, mix_lo.at(3, layer))
                        if m >= 4:
                            pe.wait_ge(split_lo.sem, split_lo.at(AT_OUT + m // 2, layer))
                            pe.wait_ge(y_copied.sem, y_copied.at(KT + m - 4, layer))
                            for kt in range(HEADS, KT):
                                three(PS[:, m % 4, 0:T], *block_of(slot, (m % 2) * KT + kt), *x_tile(kt, T),
                                      kt == HEADS, False)
                        for kt in range(HEADS):
                            ins = three(PS[:, m % 4, 0:T], *block_of(slot, (m % 2) * KT + kt), *x_tile(kt, T),
                                        False, kt == HEADS - 1)
                        ins.then_inc(products.sem, 1)

            pe.wait_ge(in_masks, 32)
            for layer in range(DEPTH):
                ffn(layer, 0)
                out_norm(layer, 0)
                mixer(layer)
                out_norm(layer, 1)
                ffn(layer, 1)
                out_norm(layer, 2)


def constants():
    at = np.arange(P)
    chunk = np.where(at < N_SAMPLE, at // SEQ_T, np.where(at < META_AT + N_META, SEQS, SEQS + 1))
    row, col = at[:, None], at[None, :]
    same = chunk[:, None] == chunk[None, :]
    found = {
        "ident": row == col, "ones": row >= 0, "incl_full": row <= col, "incl_seq": (row <= col) & same,
        "strict_full": row < col, "strict_seq": (row < col) & same, "same_seq": same,
        "pair": (row + 1 == col) & (row % 2 == 0),
    }
    for m in (2, 4, 8, 16, 32, 64):
        found[f"lv{m}"] = (row // (2 * m) == col // (2 * m)) & (row // m % 2 == 1) & (col // m % 2 == 0)
    masks = np.stack([np.broadcast_to(found[name], (P, P)) for name in MASKS], axis=1).astype(np.float32)
    ind = (chunk[:, None] == np.arange(SEQS + 1)[None, :]).astype(np.float32)
    return masks, ind


def features_first(a):
    a = a.reshape(*a.shape[:-1], a.shape[-1] // P, P)
    return np.moveaxis(a, -1, 0)


def layout(a):
    L = DEPTH
    x = np.concatenate([a["x_prompt"][0], a["x_sample"].reshape(N_SAMPLE, D_MODEL), a["meta_tokens"]])
    x = np.ascontiguousarray(x.reshape(T, KT, P).transpose(2, 1, 0))

    def in_tiles(w):
        n = w.shape[2] // P
        return w.reshape(L, KT, P, n, P).transpose(0, 3, 2, 1, 4).reshape(L, n, P, KT * P)

    def pairs(w):
        n = w.shape[1] // 2
        return w.reshape(L, n, 2, P, KT * P).transpose(0, 1, 3, 2, 4).reshape(L, n, P, A_LEN)

    up = [pairs(np.stack([in_tiles(a[f"ffn{s}_gate"]), in_tiles(a[f"ffn{s}_up"])], axis=2).reshape(L, 2 * FT, P, KT * P))
          for s in (1, 2)]
    down = [a[f"ffn{s}_down"].reshape(L, 2, DH, P, KT, P).transpose(0, 4, 1, 3, 2, 5).reshape(L, N_DOWN, P, D_LEN)
            for s in (1, 2)]
    w = a["w_in"]
    gates_at = 4 * HEADS * P
    rest = gates_at + 2 * HEADS
    tiles = np.concatenate([in_tiles(w[:, :, 0:gates_at]), in_tiles(w[:, :, rest:])], axis=1)
    order = list(range(QKV_T + 8))
    for i in range(4):
        order += [20 + i, 24 + i]
    w_8 = w[:, :, gates_at:rest].reshape(L, KT, P, 8).transpose(0, 2, 1, 3).reshape(L, P, KT * 8)
    par = np.concatenate([a["norm_gains"].reshape(L, -1, P), a["conv_gdn"].reshape(L, -1, P),
                          a["conv_sc"].reshape(L, -1, P), a["gdn_norm"].reshape(L, 1, P)], axis=1)
    masks, ind = constants()
    hist_g = a["cache_gdn_conv"].reshape(L, SEQS, G_HIST, QKV_T, P).transpose(4, 0, 3, 1, 2)
    hist_s = a["cache_sconv"].reshape(L, SEQS, S_HIST, 4, P).transpose(4, 0, 3, 1, 2)
    return {
        "x": x, "par": par.transpose(2, 0, 1), "hist_g": hist_g, "hist_s": hist_s,
        "gate_p": np.stack([a["a_log"], a["dt_bias"]], axis=1), "masks": masks, "ind": ind,
        "w_up": np.stack(up, axis=1), "w_down": np.stack(down, axis=1), "w_in": pairs(tiles[:, order]),
        "w_8": w_8, "w_out": pairs(in_tiles(a["w_out"])),
        "states": a["state_gdn"].transpose(0, 3, 1, 2, 4),
    }


OUTS = {
    "y": [P, KT, N_PROMPT + N_SAMPLE], "new_g": [DEPTH, P, QKV_T, 1 + SEQS, G_HIST],
    "new_s": [DEPTH, P, 4, 1 + SEQS, S_HIST], "state_p": [DEPTH, P, HEADS, P], "state_s": [DEPTH, P, SEQS, HEADS, P],
}


def kernel(**inputs):
    import concourse.bacc as bacc
    from concourse.bass_utils import run_bass_kernel_spmd

    nc = bacc.Bacc("TRN2", target_bir_lowering=False, num_devices=1)
    arrays, io = {}, {}
    for name, a in layout({k: np.asarray(v) for k, v in inputs.items()}).items():
        arrays[f"in_{name}"] = np.ascontiguousarray(a)
        io[name] = nc.dram_tensor(f"in_{name}", a.shape, F32, kind="ExternalInput").ap()
    for name, shape in OUTS.items():
        io[name] = nc.dram_tensor(f"out_{name}", shape, F32, kind="ExternalOutput").ap()
    decoder_trunk(nc, io)
    out = run_bass_kernel_spmd(nc, [arrays], core_ids=[0]).results[0]
    y = out["out_y"].transpose(2, 1, 0).reshape(-1, D_MODEL)
    new_g = out["out_new_g"].transpose(0, 3, 4, 2, 1).reshape(DEPTH, 1 + SEQS, G_HIST, QKV_T * P)
    new_s = out["out_new_s"].transpose(0, 3, 4, 2, 1).reshape(DEPTH, 1 + SEQS, S_HIST, 4 * P)
    state_p = out["out_state_p"].transpose(0, 2, 1, 3)[:, None]
    state_s = out["out_state_s"].transpose(0, 2, 3, 1, 4)
    return (y[None, :N_PROMPT], y[N_PROMPT:].reshape(SEQS, SEQ_T, D_MODEL), state_p, new_g[:, :1], new_s[:, :1],
            state_s, new_g[:, 1:], new_s[:, 1:])
```

```python
from contextlib import ExitStack

import numpy as np

import concourse.bass as bass
from concourse import mybir

F32 = mybir.dt.float32
F32R = mybir.dt.float32r
ALU = mybir.AluOpType
ACT = mybir.ActivationFunctionType

P = 128
DEPTH = 2
D_MODEL = 1024
KT = D_MODEL // P
HEADS = 4
N_PROMPT, N_META = 256, 16
SEQS, SEQ_T = 8, 8
N_SAMPLE = SEQS * SEQ_T
T = N_PROMPT + N_SAMPLE + N_META
TT = 3
TP = TT * P
C_TILE = 2
META_AT = N_SAMPLE
D_FF = 2816
FT = D_FF // P
DH = FT // 2
QKV_T = 12
GW, SW = 4, 3
EPS = 1e-6

G_HIST, S_HIST = GW - 1, SW - 1
G_SEQ0, S_SEQ0 = G_HIST + N_META + N_PROMPT, S_HIST + N_META + N_PROMPT
G_STEP, S_STEP = G_HIST + SEQ_T, S_HIST + SEQ_T
G_LEN, S_LEN = G_SEQ0 + SEQS * G_STEP, S_SEQ0 + SEQS * S_STEP

N_UP, N_DOWN, N_IN, N_OUT = FT, 2 * KT, 14, 4
A_LEN, D_LEN = 2 * KT * P, DH * P
AT_UP = (0, N_UP + N_DOWN + N_IN + N_OUT)
AT_DOWN = (N_UP, N_UP + N_DOWN + N_IN + N_OUT + N_UP)
AT_IN = N_UP + N_DOWN
AT_OUT = AT_IN + N_IN
CHUNKS = 2 * (N_UP + N_DOWN) + N_IN + N_OUT
PR_UP = (0, N_UP + N_DOWN + 2 * N_IN + 2 * N_OUT)
PR_DOWN = (N_UP, PR_UP[1] + N_UP)
PR_IN = N_UP + N_DOWN
PR_OUT = PR_IN + 2 * N_IN
PRODUCTS = 2 * (N_UP + N_DOWN) + 2 * N_IN + 2 * N_OUT

C_GAIN, C_CG, C_CS, C_GN = 0, 48, 96, 108
N_PAR = 109

MASKS = ["ident", "ones", "incl_full", "incl_seq", "same_seq", "pair",
         "lv2", "lv4", "lv8", "lv8_meta", "lv16", "lv32", "lv64", "pick"]
PICK_AT = 2 * HEADS - 1
LEVELS = {0: [2, 4, 8, 16, 32, 64], 1: [2, 4, 8, 16, 32, 64], 2: [2, 4, 8]}
ORDER = [2, 0, 1]
PARTS = 3
PART_KT = [(0, 3), (3, 6), (6, KT)]
LAG = 2
PER_SLOT = 2
NO_PRODUCTS = ("pair", "o_inv", "o_low", "spread")
READ_AT, OUT_AT = 38, 49


def end_of_chunk(c):
    if c < AT_IN:
        return c
    if c < AT_UP[1]:
        return PR_IN + 2 * (c - AT_IN) + 1
    return PR_UP[1] + c - AT_UP[1]


def chunk_length(c):
    return D_LEN if any(at <= c < at + N_DOWN for at in AT_DOWN) else A_LEN


def delta_stages():
    after = {("kst",): [(("vt", C_TILE), LAG)]}
    for n, t in enumerate(ORDER):
        levels = LEVELS[t]
        after["vt", t] = []
        after["pair", t] = []
        after["nt", t] = [(("pair", t), LAG)]
        for m in levels:
            after["x", t, m] = [(("nt", t) if m == 2 else ("yt", t, m // 2), LAG)]
            after["yt", t, m] = [(("x", t, m), LAG)]
        after["kt", t] = [(("x", t, levels[-1]), 1)]
        if n > 0:
            after["ks", t] = [(("st", ORDER[n - 1]), LAG), (("vt", t), LAG)]
        read = ("ks", t) if n > 0 else ("kst",)
        after["nv", t] = [(("yt", t, levels[-1]), LAG), (read, LAG), (("vt", t), LAG)]
        after["o", t] = [(("nv", t), LAG), (("kt", t), LAG)]
        after["st", t] = [(("o", t), 0), (("kt", t), LAG)]
        after["o_cols", t] = [(("o", t), LAG)]
        after["o_inv", t] = [(("o_cols", t), LAG)]
        after["rob", t] = [(("o_inv", t), 1)]
        after["o_low", t] = [(("rob", t), 1)]
    after["st", C_TILE] = [(("nv", C_TILE), LAG), (("kt", C_TILE), LAG)]
    pairs = [(h, half) for h in range(HEADS) for half in range(2)]
    for k, (h, half) in enumerate(pairs):
        after["spread", h, half] = [(("o", C_TILE), LAG)]
        after["sn", h, half] = [(("spread", h, half), 1)]
        if k > 0:
            after["spread", h, half].append((("spread", *pairs[k - 1]), 1))
            after["sn", h, half].append((("sn", *pairs[k - 1]), 1))
        if k > 1:
            after["spread", h, half].append((("sn", *pairs[k - 2]), 1))
    return after


def mixer_steps():
    tiles, first = 2 * N_IN, 4
    end = (tiles - first) * PARTS
    steps = [("entry",), ("hi", 0, 0), ("hi", 0, 1), ("lo", 0), ("evac", 0), ("evac", 1), ("tap", 0), ("tap", 1),
             ("gate_rows",), ("evac", 2), ("evac", 3)]
    slot_work = [[] for _ in range(end)]
    slot_work[0] += [("gate_cols",), ("hi", 1, 0), ("conv", 0), ("hi", 1, 1)]
    slot_work[1] += [("gate_g",), ("lo", 1), ("conv", 1)]
    slot_work[2] += [("cum",)]
    slot_work[3] += [("gb", ORDER[0]), ("gb", ORDER[1])]
    slot_work[4] += [("gb", ORDER[2])]
    slot_work[5] += [("silu", 0), ("tap", 2), ("conv", 2), ("silu", 1), ("tap", 3)]
    slot_work[6] += [("sq", 0), ("conv", 3), ("sq", 1)]
    slot_work[7] += [("silu", 2)]
    slot_work[8] += [("sq_rows", 0), ("silu", 3), ("sq", 2)]
    slot_work[9] += [("sq_rows", 1), ("sq", 3)]
    slot_work[10] += [("sq_rows", 2)]
    slot_work[11] += [("sq_rows", 3)]
    conv_at = {i: 8 + (7 * (i - 4)) // 3 for i in range(4, QKV_T)}
    for i, at in conv_at.items():
        slot_work[at] += [("tap", i), ("conv", i)]
        slot_work[at + 1].append(("silu", i))
        if i < 2 * HEADS:
            slot_work[at + 2].append(("sq", i))
            slot_work[at + 4].append(("sq_rows", i))
    scores_at = conv_at[2 * HEADS - 1] + 6
    slot_work[scores_at - 1].append(("sq_cols",))
    slot_work[scores_at].append(("norms",))
    for n, t in enumerate(ORDER):
        slot_work[scores_at + 2 * n].append(("qk", t))
        slot_work[scores_at + 2 * n + 1].append(("kk", t))
    for i in range(QKV_T + 4, tiles - 1):
        if (i - QKV_T - 8) % 2:
            slot_work[(i + 1 - first) * PARTS] += [("tap", i), ("conv", i)]
    z_at = (QKV_T + 4 - first) * PARTS
    slot_work[z_at] += [("silu", QKV_T), ("silu", QKV_T + 1)]
    slot_work[z_at + 1] += [("silu", QKV_T + 2), ("silu", QKV_T + 3), ("key_norms",)]
    for i in range(first, tiles - 1):
        if i % 2:
            at = (i + 1 - first) * PARTS
            slot_work[at].insert(0, ("hi", i // 2, 0))
            slot_work[at + 1].insert(0, ("hi", i // 2, 1))
            slot_work[at + 2].append(("lo", i // 2))
    for h in range(HEADS):
        slot_work[READ_AT + h].append(("ksT", h))
        slot_work[OUT_AT + h].append(("oC", h))

    after = delta_stages()
    followers = {name: [] for name in after}
    for name, before in after.items():
        for other, lag in before:
            followers[other].append((name, lag))
    earliest = {("vt", t): z_at + 3 for t in ORDER}
    earliest.update({("pair", t): conv_at[QKV_T - 1] + 2 for t in ORDER})
    earliest["kst",] = READ_AT + HEADS + LAG
    earliest["o", C_TILE] = OUT_AT + HEADS
    latest = {("nv", C_TILE): OUT_AT - LAG}

    def path(name):
        return max([path(other) + max(lag, 1) for other, lag in followers[name]], default=0)

    left = sorted(after, key=lambda name: -path(name))
    at = {}

    def fill(now):
        chosen, products = [], 0
        for name in list(left):
            if products + (name[0] not in NO_PRODUCTS) <= PER_SLOT and now >= earliest.get(name, 0) and \
                    all(other in at and at[other] + lag <= now for other, lag in after[name]):
                chosen.append([name])
                products += name[0] not in NO_PRODUCTS
                if name[0] == "yt" and name[2] != LEVELS[name[1]][-1]:
                    chosen[-1].insert(0, ("y",) + name[1:])
                assert now <= latest.get(name, now), name
                at[name] = now
                left.remove(name)
        return chosen

    for now in range(end):
        i, p = first + now // PARTS, now % PARTS
        steps.append(("part", i, p))
        if p == PARTS - 1:
            steps.append(("evac", i))
        fillers = fill(now)
        steps += sum(fillers[:1], []) + slot_work[now] + sum(fillers[1:], [])
    now, tail = end, [("finish",)]
    while left:
        assert now < end + 20
        steps += sum(fill(now), [])
        if tail:
            steps.append(tail.pop())
        now += 1
    steps += tail + [("out_o", m) for m in range(4)]
    return steps + [("out", m) for m in range(KT)]


EVACUATED_BY = {
    "gate_rows": "dve", "cum": "act", "gb": "act", "qk": "dve", "kk": "dve", "vt": "act", "nt": "act", "x": "dve", "y": "dve",
    "yt": "dve", "kt": "act", "kst": "dve", "nv": "dve", "ks": "dve", "o": "act", "st": "dve", "rob": "dve",
    "sn": "dve",
}


def delta_groups():
    order, left_psum, n = [], {}, {"dve": 0, "act": 0}
    for step in mixer_steps():
        if step[0] in EVACUATED_BY and step != ("o", C_TILE):
            order.append(step)
            engine = EVACUATED_BY[step[0]]
            left_psum[step] = (engine, n[engine])
            n[engine] += 1
    return order, left_psum, n


class Signal:

    def __init__(self, sem, per_layer=0, by=1):
        self.sem, self.per, self.by = sem, per_layer, by

    def at(self, n, layer=0):
        return (layer * self.per + n + 1) * self.by


class Chain:

    def __init__(self, engine, sem):
        self.engine, self.sem, self.n = engine, sem, 0

    def step(self, ins):
        ins.then_inc(self.sem, 1)
        self.n += 1
        self.engine.wait_ge(self.sem, self.n)


def decoder_trunk(nc, io):
    ctx = ExitStack()
    with ctx:
        cursor = [(nc.sbuf_base + 63) // 64 * 64]

        def place(name, shape, dt, at):
            return nc.alloc_sbuf_tensor_at(name, shape, dt, offset=at)

        def region(nbytes):
            at = cursor[0]
            cursor[0] = (at + nbytes + 31) // 32 * 32
            return at

        def size(shape):
            return int(np.prod(shape[1:])) * 4

        def sb(name, shape, dt=F32):
            return place(name, shape, dt, region(size(shape)))

        def stack(at, *specs):
            out = []
            for name, shape, dt in specs:
                out.append(place(name, shape, dt, at))
                at += (size(shape) + 31) // 32 * 32
            return out, at

        X = sb("X", [P, KT, T])
        XH = sb("XH", [P, KT, TP], F32R)
        XL = sb("XL", [P, KT, TP], F32R)
        RAW = [sb(f"RAW{i}", [P, A_LEN]) for i in range(2)]
        WH = [sb(f"WH{i}", [P, A_LEN], F32R) for i in range(2)]
        WL = [sb(f"WL{i}", [P, A_LEN], F32R) for i in range(2)]
        W8R = sb("W8R", [P, KT * 8])
        W8H = sb("W8H", [P, KT * 8], F32R)
        W8L = sb("W8L", [P, KT * 8], F32R)
        SEQ_S = sb("SEQ_S", [P, SEQS, HEADS, P])
        PR_S = sb("PR_S", [P, HEADS, P])
        PAR_ALL = sb("PAR_ALL", [P, DEPTH, N_PAR])
        HALF_G = sb("HALF_G", [P, DEPTH, 2, KT])
        EPSC = sb("EPSC", [P, 2])
        HIST_G = sb("HIST_G", [P, DEPTH, QKV_T, SEQS, G_HIST])
        HIST_S = sb("HIST_S", [P, DEPTH, 4, SEQS, S_HIST])
        GATE_P = sb("GATE_P", [P, DEPTH, 2, HEADS])
        MK = sb("MK", [P, len(MASKS), P])
        IND = sb("IND", [P, SEQS + 1])
        RB = sb("RB", [P, T])
        SQX = [sb(f"SQX{i}", [P, TP]) for i in range(2)]
        SQY = [sb(f"SQY{i}", [P, T]) for i in range(2)]
        ACCX = sb("ACCX", [P, TP])
        ACCY = sb("ACCY", [P, TP])
        TMP = [sb(f"TMP{i}", [P, T]) for i in range(2)]
        RC = sb("RC", [P, 4, TT])
        NEW_G = sb("NEW_G", [P, QKV_T, 1 + SEQS, G_HIST])
        NEW_S = sb("NEW_S", [P, 4, 1 + SEQS, S_HIST])
        TOK = sb("TOK", [P, 16, TT, HEADS])
        B8 = sb("B8", [P, TT, 2 * HEADS])
        NEG_A = sb("NEG_A", [P, DEPTH, HEADS])
        SEQ_EL = sb("SEQ_EL", [P, HEADS, SEQS + 1])
        SEQ_GB = sb("SEQ_GB", [P, HEADS, SEQS + 1])
        SSQ = sb("SSQ", [P, TT, 2 * HEADS])

        h_at = region(2 * FT * T * 4)
        (HH, HL), h_end = stack(h_at, ("HH", [P, FT, T], F32R), ("HL", [P, FT, T], F32R))
        (EXT,), at = stack(h_at, ("EXT", [P, QKV_T, G_LEN], F32))
        (NI, MI, XM0, XM1), e_end = stack(h_at, ("NI", [P, TT, HEADS, P], F32), ("MI", [P, TT, HEADS, P], F32),
                                          ("XM0", [P, HEADS, P], F32), ("XM1", [P, HEADS, P], F32))
        assert e_end <= at
        (OH, _, OL), _ = stack(at, ("OH", [P, HEADS, TP], F32R), ("OV", [P, HEADS, TP], F32),
                                  ("OL", [P, HEADS, TP], F32R))
        (QKV, UEXT, ZS, BY, QKM), at = stack(
            at, ("QKV", [P, QKV_T, TP], F32), ("UEXT", [P, 4, S_LEN], F32), ("ZS", [P, HEADS, T], F32),
            ("BY", [P, 4, T], F32), ("QKM", [P, TT, HEADS, P], F32))
        assert at <= h_end, (at - h_at, h_end - h_at)
        g_at = region(8 * T * 4)
        (GR0, GR1, UR0, UR1, SG0, SG1, HF0, HF1), g_end = stack(
            g_at, *[(f"{n}{i}", [P, T], F32) for n in ("GR", "UR", "SG", "HF") for i in range(2)])
        GR, UR, SG, HF = [GR0, GR1], [UR0, UR1], [SG0, SG1], [HF0, HF1]
        (VS, CV0, CV1, RB2), at = stack(g_at, ("VS", [P, TT, HEADS, P], F32), ("CV0", [P, G_LEN], F32),
                                   ("CV1", [P, G_LEN], F32), ("RB2", [P, T], F32))
        CV = [CV0, CV1]
        assert at <= g_end
        y_at = region(KT * T * 4)
        (Y,), y_end = stack(y_at, ("Y", [P, KT, T], F32))
        (DA, EGB, KST), at = stack(y_at, ("DA", [P, TT, HEADS, P], F32), ("EGB", [P, HEADS, P], F32),
                                   ("KST", [P, HEADS, P], F32))
        assert at <= y_end
        assert cursor[0] <= nc.sbuf_usable_end, (cursor[0], nc.sbuf_usable_end)
        XB = {0: XM0[:, :, :], 1: XM1[:, :, :], 2: EGB[:, :, :]}
        NVP, KTL = DA, NI

        PS = ctx.enter_context(nc.psum_tensor("PS", [P, 8, 512], F32))
        GROUP_ORDER, LEFT_PSUM, N_EVAC = delta_groups()
        GROUP_INDEX = {name: n for n, name in enumerate(GROUP_ORDER)}

        def sig(name, per, by=1):
            return Signal(ctx.enter_context(nc.semaphore(name)), per, by)

        def sem(name):
            return ctx.enter_context(nc.semaphore(name))

        in_x = [sem(f"in_x{m}") for m in range(KT)]
        in_par, in_masks, in_hist, in_gate = sem("in_par"), sem("in_masks"), sem("in_hist"), sem("in_gate")
        zeroed, eps_set, gate_exp = sem("zeroed"), sem("eps_set"), sem("gate_exp")
        raw_in = [sig(f"raw_in{i}", CHUNKS // 2, 16) for i in range(2)]
        w8_in, states_in = sig("w8_in", 1, 16), sig("states_in", 1, 16)
        w8_hi, w8_lo = sig("w8_hi", 1), sig("w8_lo", 1)
        split_hi, split_lo = sig("split_hi", CHUNKS), sig("split_lo", CHUNKS)
        split_lo2 = sig("split_lo2", N_IN)
        products = sig("products", PRODUCTS)
        x_hi, x_lo, x_sq, x_acc, x_new = (sig(n, 3 * KT) for n in ("x_hi", "x_lo", "x_sq", "x_acc", "x_new"))
        y_copied, y_sq, y_acc = (sig(n, 3 * KT) for n in ("y_copied", "y_sq", "y_acc"))
        x_cols, x_root, x_inv, x_rows, x_rb = (sig(n, 3) for n in ("x_cols", "x_root", "x_inv", "x_rows", "x_rb"))
        y_cols, y_root, y_inv, y_rows = (sig(n, 3) for n in ("y_cols", "y_root", "y_inv", "y_rows"))
        gate_scaled, up_scaled, silu_done, h_full, h_hi, h_lo = (
            sig(n, 2 * FT) for n in ("gate_scaled", "up_scaled", "silu_done", "h_full", "h_hi", "h_lo"))
        hist_set = sig("hist_set", 1)
        proj_read = sig("proj_read", 2 * N_IN)
        tap0, conv_done = sig("tap0", QKV_T + 4), sig("conv_done", QKV_T)
        act_out = sig("act_out", QKV_T + 4)
        qk_sq, sq_summed = sig("qk_sq", 2 * HEADS), sig("sq_summed", 2 * HEADS)
        sq_out, qk_cols = sig("sq_out", 1), sig("qk_cols", 1)
        mix_y, mix_hi, mix_lo = sig("mix_y", 4), sig("mix_hi", 1), sig("mix_lo", 1)
        o_hi, o_lo = sig("o_hi", TT), sig("o_lo", TT)
        qk_masked, q_decayed = sig("qk_masked", TT), sig("q_decayed", TT)
        seq_read, seq_keys, seq_out = sig("seq_read", 1), sig("seq_keys", 1), sig("seq_out", 1)
        new_hist = sig("new_hist", 2)
        key_norm, seq_copied = sig("key_norm", 1), sig("seq_copied", 1)
        small = sig("small", 1 + TT)
        to_act, to_dve = sig("to_act", 3 + TT), sig("to_dve", 1 + TT)
        gate_g = sig("gate_g", 1)
        dd_raw, dd_exp = sig("dd_raw", TT), sig("dd_exp", TT)
        pair_set = sig("pair_set", TT)
        filled = sig("filled", len(GROUP_ORDER))
        evac = {"dve": sig("evac_dve", N_EVAC["dve"]), "act": sig("evac_act", N_EVAC["act"])}
        kst_zero = sig("kst_zero", 1)
        seq_spread = sig("seq_spread", 2 * HEADS)
        o_inv, o_full = sig("o_inv", TT), sig("o_full", TT)
        states_out, hist_out = sig("states_out", 2, 16), sig("hist_out", 2, 16)
        out_sem = sem("out_sem")
        chain_dve, chain_act = sem("chain_dve"), sem("chain_act")

        def mask(name, width=P):
            return MK[:, MASKS.index(name), 0:width]

        def heads_of(ap):
            return ap.unsqueeze(1).to_broadcast([P, HEADS, P])

        def per_head(tok):
            return tok.unsqueeze(2).to_broadcast([P, HEADS, P])

        def incl(t):
            return mask("incl_seq" if t == C_TILE else "incl_full")

        def bank(i):
            return PS[:, i, :]

        def heads_bank(name):
            return PS[:, 5 + GROUP_INDEX[name] % 3, :].rearrange("p (h n) -> p h n", h=HEADS)

        def blocks(ap, m, parity):
            if len(ap.shape) == 2:
                return ap.rearrange("p (b two m) -> p b two m", two=2, m=m)[:, :, parity, :]
            return ap.rearrange("p h (b two m) -> p h b two m", two=2, m=m)[:, :, :, parity, :]

        GATE_ROWS = PS[0:2 * HEADS, 5 + GROUP_INDEX["gate_rows",] % 3, 0:T]
        SQ_ROWS = PS[0:2 * HEADS, 4, P:P + T]
        P8 = PS[:, 4, 0:24].rearrange("p (t c) -> p t c", t=TT)
        CUM = PS[:, 5 + GROUP_INDEX["cum",] % 3, :]
        GCOL = CUM[:, 24:36].rearrange("p (t h) -> p t h", t=TT)
        GLAST = CUM[:, 36:48].rearrange("p (t h) -> p t h", t=TT)
        SEQ_GL = CUM[:, 48:84].rearrange("p (h s) -> p h s", h=HEADS)
        QK_COLS = PS[:, 4, 24:48].rearrange("p (t c) -> p t c", t=TT)
        O_COLS = PS[:, 4, 48:60].rearrange("p (t h) -> p t h", t=TT)
        Y_COLS, X_COLS = PS[:, 4, 64:67], PS[:, 4, 68:71]
        Y_ROWS, X_ROWS = PS[:, 5, 0:T], PS[:, 6, 0:T]
        (BETA, G, GC, EG, NEG_EG, KTS, EL, NK, CK, WQ, RO, T0, T1, T2, T3, T4) = (TOK[:, i, :, :] for i in range(16))

        def qT(cols):
            return QKV[:, 0:HEADS, cols]

        def kT(cols):
            return QKV[:, HEADS:2 * HEADS, cols]

        def vT(cols):
            return QKV[:, 2 * HEADS:3 * HEADS, cols]

        def tcols(t):
            return slice(t * P, (t + 1) * P)

        def gain(layer, j, after, m):
            if after and j != 1:
                return HALF_G[:, layer, j // 2, m:m + 1]
            at = C_GAIN + KT * (2 * j + after) + m
            return PAR_ALL[:, layer, at:at + 1]

        def proj_bank(i):
            return i if i < 4 else (i - 4) % 3

        STEPS = mixer_steps()
        SEQ_G = SEQ_GB[:, :, :]
        SEQ_READ = PS[:, 3, :].rearrange("p (h n) -> p h n", h=HEADS)
        NTH = {step: sum(other[0] == step[0] for other in STEPS[:n]) for n, step in enumerate(STEPS)}
        SEQ_NAMES = [name for name in GROUP_ORDER if name[0] == "sn"]
        SEQ_BUF = [EGB, KST]
        PROJ = [("qkv", i) for i in range(QKV_T)] + [("z", i) for i in range(4)] + [("b", i) for i in range(4)]
        for i in range(4):
            PROJ += [("c", i), ("h", i)]


        block = ctx.enter_context(nc.Block())

        def raw_value(layer, c):
            return raw_in[0].at(c // 2, layer)

        def tokens(f):
            return T if f < 2 * DEPTH - 1 else N_PROMPT + N_SAMPLE

        def hidden(buf, c, n):
            return buf[:, bass.ds(c, 1), 0:n].rearrange("p a t -> p (a t)") if not isinstance(c, int) else buf[:, c, 0:n]

        def seqs(ap):
            return ap.rearrange("p (s t) -> p s t", s=SEQS)

        @block.sync
        def _(sp):
            for m in range(KT):
                sp.dma_start(X[:, m, :], io["x"][:, m, :]).then_inc(in_x[m], 16)
                if m == 0:
                    sp.dma_start(PAR_ALL[:, :, :], io["par"]).then_inc(in_par, 16)
                if m == 1:
                    for slot in range(2):
                        sp.dma_start(RAW[slot][:, :], io["w_up"][0, 0, slot]).then_inc(raw_in[slot].sem, 16)
                    sp.dma_start(W8R[:, :], io["w_8"][0]).then_inc(w8_in.sem, 16)
            sp.dma_start(MK[:, :, :], io["masks"]).then_inc(in_masks, 16)
            sp.dma_start(IND[:, :], io["ind"]).then_inc(in_masks, 16)
            sp.dma_start(HIST_G[:, :, :, :, :], io["hist_g"]).then_inc(in_hist, 16)
            sp.dma_start(HIST_S[:, :, :, :, :], io["hist_s"]).then_inc(in_hist, 16)
            sp.dma_start(GATE_P[:, :, :, :], io["gate_p"].partition_broadcast(P)).then_inc(in_gate, 16)

            def run(layer, at, n, src, length, skip=0):
                with sp.Fori(0, n // 2 - skip) as i:
                    for slot in range(2):
                        sp.wait_ge(split_lo.sem, split_lo.at(at + 2 * skip + 2 * i + slot - 2, layer))
                        sp.dma_start(RAW[slot][:, 0:length], src(2 * i + 2 * skip + slot)).then_inc(raw_in[slot].sem, 16)

            def row(table, c):
                return table[bass.ds(c, 1)].rearrange("a p n -> (a p) n")

            for layer in range(DEPTH):
                if layer > 0:
                    sp.wait_ge(w8_lo.sem, w8_lo.at(0, layer - 1))
                    sp.dma_start(W8R[:, :], io["w_8"][layer]).then_inc(w8_in.sem, 16)
                    sp.wait_ge(states_out.sem, states_out.at(1, layer - 1))
                sp.dma_start(SEQ_S[:, :, :, :], io["states"][layer]).then_inc(states_in.sem, 16)
                run(layer, AT_UP[0], N_UP, lambda c: row(io["w_up"][layer, 0], c), A_LEN, skip=1 if layer == 0 else 0)
                run(layer, AT_DOWN[0], N_DOWN, lambda c: row(io["w_down"][layer, 0], c), D_LEN)
                run(layer, AT_IN, 4, lambda c: row(io["w_in"][layer], c), A_LEN)
                for c in range(4, N_IN + N_OUT):
                    sp.wait_ge(split_lo.sem, split_lo.at(AT_IN + c - 2, layer))
                    sp.wait_ge(split_lo2.sem, split_lo2.at(c - 4, layer))
                    src = io["w_in"][layer, c] if c < N_IN else io["w_out"][layer, c - N_IN]
                    sp.dma_start(RAW[c % 2][:, :], src).then_inc(raw_in[c % 2].sem, 16)
                run(layer, AT_UP[1], N_UP, lambda c: row(io["w_up"][layer, 1], c), A_LEN)
                run(layer, AT_DOWN[1], N_DOWN, lambda c: row(io["w_down"][layer, 1], c), D_LEN)

        @block.gpsimd
        def _(pool):
            for buf in (XH, XL):
                pool.memset(buf[:, :, T:TP].bitcast(F32), 0.0)
            for buf in (*SQX, ACCX):
                pool.memset(buf[:, T:TP], 0.0)
            pool.memset(ACCY[:, T:TP], 0.0).then_inc(zeroed, 1)

            def add_squares(layer, j):
                for m in range(KT):
                    pool.wait_ge(x_sq.sem, x_sq.at(j * KT + m, layer))
                    if m == 0:
                        if (layer, j) != (0, 0):
                            pool.wait_ge(x_cols.sem, x_cols.at(j - 1 if j else 2, layer if j else layer - 1))
                        ins = pool.tensor_copy(ACCX[:, 0:T], SQX[0][:, 0:T])
                    else:
                        pool.wait_ge(x_acc.sem, x_acc.at(j * KT + m - 1, layer))
                        ins = pool.tensor_tensor(ACCX[:, 0:T], ACCX[:, 0:T], SQX[m % 2][:, 0:T], ALU.add)
                    ins.then_inc(x_acc.sem, 1)

            add_squares(0, 0)
            pool.wait_ge(in_hist, 32)
            for layer in range(DEPTH):
                pool.wait_ge(y_acc.sem, y_acc.at(KT - 1, layer))
                pool.memset(EXT[:, :, 0:G_HIST], 0.0)
                pool.memset(UEXT[:, :, 0:S_HIST], 0.0)
                pool.memset(QKV[:, :, T:TP], 0.0)
                for i in range(QKV_T):
                    pool.tensor_copy(seqs(EXT[:, i, G_SEQ0:])[:, :, 0:G_HIST], HIST_G[:, layer, i, :, :])
                for i in range(4):
                    ins = pool.tensor_copy(seqs(UEXT[:, i, S_SEQ0:])[:, :, 0:S_HIST], HIST_S[:, layer, i, :, :])
                ins.then_inc(hist_set.sem, 1)
                add_squares(layer, 1)
                pool.wait_ge(x_new.sem, x_new.at(KT - 1, layer))
                pool.memset(KST[:, :, :], 0.0).then_inc(kst_zero.sem, 1)
                if layer > 0:
                    pool.wait_ge(hist_out.sem, hist_out.at(1, layer - 1))
                for step in STEPS:
                    what, t = step[0], step[-1]
                    if what == "lo":
                        slot, cols = t % 2, slice(A_LEN // 2, A_LEN)
                        pool.wait_ge(split_hi.sem, split_hi.at(AT_IN + t + 2, layer))
                        pool.tensor_tensor(WL[slot][:, cols], RAW[slot][:, cols], WH[slot][:, cols].bitcast(F32),
                                           ALU.subtract).then_inc(split_lo2.sem, 1)
                    elif what == "evac" and t < QKV_T:
                        pool.wait_ge(proj_read.sem, proj_read.at(t, layer))
                        pool.tensor_copy(NEW_G[:, t, 0, :], EXT[:, t, G_SEQ0 - G_HIST:G_SEQ0])
                        ins = pool.tensor_copy(NEW_G[:, t, 1:, :], seqs(EXT[:, t, G_SEQ0:])[:, :, SEQ_T:])
                        if t == QKV_T - 1:
                            ins.then_inc(new_hist.sem, 1)
                            pool.wait_ge(new_hist.sem, new_hist.at(0, layer))
                            pool.dma_start(io["new_g"][layer], NEW_G[:, :, :, :]).then_inc(hist_out.sem, 16)
                    elif what == "kk":
                        pool.wait_ge(evac["dve"].sem, evac["dve"].at(LEFT_PSUM["qk", t][1], layer))
                        pool.tensor_tensor(QKM[:, t, :, :], QKM[:, t, :, :], heads_of(incl(t)),
                                           ALU.mult).then_inc(qk_masked.sem, 1)
                    elif what == "evac" and PROJ[t][0] == "h":
                        n = PROJ[t][1]
                        pool.wait_ge(proj_read.sem, proj_read.at(t, layer))
                        pool.tensor_copy(NEW_S[:, n, 0, :], UEXT[:, n, S_SEQ0 - S_HIST:S_SEQ0])
                        ins = pool.tensor_copy(NEW_S[:, n, 1:, :], seqs(UEXT[:, n, S_SEQ0:])[:, :, SEQ_T:])
                        if n == 3:
                            ins.then_inc(new_hist.sem, 1)
                            pool.wait_ge(new_hist.sem, new_hist.at(1, layer))
                            pool.dma_start(io["new_s"][layer], NEW_S[:, :, :, :]).then_inc(hist_out.sem, 16)
                    elif what == "finish":
                        slot, cols = (N_IN - 1) % 2, slice(A_LEN // 2, A_LEN)
                        pool.wait_ge(split_hi.sem, split_hi.at(AT_OUT + 1, layer))
                        pool.tensor_tensor(WL[slot][:, cols], RAW[slot][:, cols], WH[slot][:, cols].bitcast(F32),
                                           ALU.subtract).then_inc(split_lo2.sem, 1)
                pool.wait_ge(evac["dve"].sem, evac["dve"].at(LEFT_PSUM["st", 1][1], layer))
                pool.dma_start(io["state_p"][layer], PR_S[:, :, :]).then_inc(states_out.sem, 16)
                pool.wait_ge(evac["dve"].sem, evac["dve"].at(LEFT_PSUM[SEQ_NAMES[-1]][1], layer))
                pool.dma_start(io["state_s"][layer], SEQ_S[:, :, :, :]).then_inc(states_out.sem, 16)
                add_squares(layer, 2)
                if layer + 1 < DEPTH:
                    add_squares(layer + 1, 0)
            for m in range(KT):
                pool.wait_ge(x_new.sem, x_new.at(2 * KT + m, DEPTH - 1))
                pool.dma_start(io["y"][:, m, :], X[:, m, 0:N_PROMPT + N_SAMPLE]).then_inc(out_sem, 16)
            pool.wait_ge(out_sem, 16 * KT)
            pool.wait_ge(states_out.sem, states_out.at(1, DEPTH - 1))
            pool.wait_ge(hist_out.sem, hist_out.at(1, DEPTH - 1))

        @block.scalar
        def _(act):
            ch = Chain(act, chain_act)

            def split_high(slot, length, landed, used=None):
                act.wait_ge(raw_in[slot].sem, landed)
                if used is not None:
                    act.wait_ge(products.sem, used)
                act.activation(WH[slot][:, 0:length], RAW[slot][:, 0:length], ACT.Copy).then_inc(split_hi.sem, 1)

            def split_after(layer, c):
                nxt, at = (layer, c + 2) if c + 2 < CHUNKS else (layer + 1, c + 2 - CHUNKS)
                if nxt < DEPTH:
                    split_high(c % 2, chunk_length(at), raw_value(nxt, at), products.at(end_of_chunk(c), layer))

            def prenorm(layer, j, m):
                if (layer, j) == (0, 0):
                    act.wait_ge(in_x[m], 16)
                    if m == 0:
                        act.wait_ge(in_par, 16)
                        act.wait_ge(zeroed, 1)
                else:
                    act.wait_ge(x_new.sem, x_new.at((j - 1) * KT + m, layer))
                act.activation(XH[:, m, 0:T], X[:, m, :], ACT.Copy, scale=gain(layer, j, 0, m)).then_inc(x_hi.sem, 1)
                if m >= 2:
                    act.wait_ge(x_acc.sem, x_acc.at(j * KT + m - 2, layer))
                act.activation(SQX[m % 2][:, 0:T], X[:, m, :], ACT.Square).then_inc(x_sq.sem, 1)

            def x_norm(layer, j):
                act.wait_ge(x_cols.sem, x_cols.at(j, layer))
                act.activation(RC[:, 2, :], X_COLS, ACT.Sqrt, bias=EPSC[:, 0:1], scale=1.0 / D_MODEL).then_inc(x_root.sem, 1)

            def out_squares(layer, j, m, b, n, acc_value):
                act.wait_ge(y_copied.sem, y_copied.at(j * KT + m, layer))
                if acc_value is not None:
                    act.wait_ge(y_acc.sem, acc_value)
                act.activation(SQY[b][:, 0:n], hidden(Y, m, n), ACT.Square).then_inc(y_sq.sem, 1)

            def boundary(layer, j):
                act.wait_ge(y_cols.sem, y_cols.at(j, layer))
                act.activation(RC[:, 0, :], Y_COLS, ACT.Sqrt, bias=EPSC[:, 0:1], scale=1.0 / D_MODEL).then_inc(y_root.sem, 1)
                nxt = (layer, j + 1) if j < 2 else (layer + 1, 0)
                if nxt[0] < DEPTH:
                    for m in range(KT):
                        prenorm(*nxt, m)
                    x_norm(*nxt)

            def ffn(layer, s):
                j, n = 2 * s, tokens(2 * layer + s)

                def up_tile(c, k):
                    act.wait_ge(gate_scaled.sem, gate_scaled.at(s * FT + c, layer))
                    act.activation(SG[k][:, 0:n], GR[k][:, 0:n], ACT.Silu).then_inc(silu_done.sem, 1)
                    act.wait_ge(h_full.sem, h_full.at(s * FT + c, layer))
                    act.activation(hidden(HH, c, n), HF[k][:, 0:n], ACT.Copy).then_inc(h_hi.sem, 1)

                with act.Fori(0, N_UP // 2 - 1) as i:
                    for k in range(2):
                        split_high(k, A_LEN, raw_in[k].at(AT_UP[s] // 2 + i + 1, layer),
                                   products.at(PR_UP[s] + 2 * i + k, layer))
                        up_tile(2 * i + k, k)
                for k in range(2):
                    c = N_UP - 2 + k
                    split_after(layer, AT_UP[s] + c)
                    up_tile(c, k)
                act.preload_act_table(ACT.Sqrt)

                def squares(m, b, old):
                    out_squares(layer, j, m, b, n, y_acc.at(j * KT + m - 2, layer) if old else None)

                for b in range(2):
                    for k in range(2):
                        split_after(layer, AT_DOWN[s] + 2 * b + k)
                    squares(b, b, False)
                with act.Fori(1, KT // 2 - 1) as i:
                    for b in range(2):
                        for k in range(2):
                            split_high(k, D_LEN, raw_in[k].at(AT_DOWN[s] // 2 + 2 * i + b + 1, layer),
                                       products.at(PR_DOWN[s] + 4 * i + 2 * b + k, layer))
                        squares(2 * i + b, b, True)
                for b in range(2):
                    m = KT - 2 + b
                    split_after(layer, AT_DOWN[s] + 2 * m)
                    if b == 0:
                        split_after(layer, AT_DOWN[s] + 2 * m + 1)
                    squares(m, b, True)
                split_after(layer, AT_DOWN[s] + 2 * KT - 1)

            def split_half(layer, c, half):
                cols = slice(half * A_LEN // 2, (half + 1) * A_LEN // 2)
                if half == 0:
                    act.wait_ge(raw_in[c % 2].sem, raw_value(layer, c + 2))
                    act.wait_ge(products.sem, products.at(end_of_chunk(c), layer))
                ins = act.activation(WH[c % 2][:, cols], RAW[c % 2][:, cols], ACT.Copy)
                if half == 1:
                    ins.then_inc(split_hi.sem, 1)

            def tap0_of(layer, i):
                kind, n = PROJ[i]
                if kind not in ("qkv", "h"):
                    return
                act.wait_ge(proj_read.sem, proj_read.at(i, layer))
                if kind == "qkv":
                    act.wait_ge(hist_set.sem, hist_set.at(0, layer))
                    if n >= 2:
                        act.wait_ge(act_out.sem, act_out.at(n - 2, layer))
                    act.activation(CV[n % 2][:, 0:G_LEN - 3], EXT[:, n, 0:G_LEN - 3], ACT.Copy,
                                   scale=PAR_ALL[:, layer, C_CG + n:C_CG + n + 1]).then_inc(tap0.sem, 1)
                    return
                if n >= 2:
                    act.wait_ge(mix_y.sem, mix_y.at(n - 2, layer))
                else:
                    act.wait_ge(act_out.sem, act_out.at(QKV_T - 2 + n, layer))
                act.activation(CV[n % 2][:, 0:S_LEN - 2], UEXT[:, n, 0:S_LEN - 2], ACT.Copy,
                               scale=PAR_ALL[:, layer, C_CS + n:C_CS + n + 1]).then_inc(tap0.sem, 1)

            def silu(layer, i):
                kind, n = PROJ[i]
                if kind == "z":
                    act.wait_ge(proj_read.sem, proj_read.at(i, layer))
                    act.activation(ZS[:, n, :], ZS[:, n, :], ACT.Silu).then_inc(act_out.sem, 1)
                elif kind == "qkv":
                    cv = CV[n % 2]
                    act.wait_ge(conv_done.sem, conv_done.at(n, layer))
                    act.activation(QKV[:, n, 0:N_PROMPT], cv[:, N_META:N_META + N_PROMPT], ACT.Silu)
                    act.activation(QKV[:, n, N_PROMPT + N_SAMPLE:T], cv[:, 0:N_META], ACT.Silu)
                    act.activation(seqs(QKV[:, n, N_PROMPT:N_PROMPT + N_SAMPLE]),
                                   seqs(cv[:, G_SEQ0:])[:, :, 0:SEQ_T], ACT.Silu).then_inc(act_out.sem, 1)

            def evacuated(ins):
                ins.then_inc(evac["act"].sem, 1)

            def group(name, layer):
                act.wait_ge(filled.sem, filled.at(GROUP_INDEX[name], layer))
                return heads_bank(name)

            def scaled_copy(dst, name, layer, scale):
                src = group(name, layer)
                for h in range(HEADS):
                    ins = act.activation(dst[:, h, :], src[:, h, :], ACT.Copy, scale=scale[:, h:h + 1])
                evacuated(ins)

            def mixer(layer):
                for step in STEPS:
                    what, t = step[0], step[-1]
                    if what == "tap":
                        tap0_of(layer, t)
                    elif what == "silu":
                        silu(layer, t)
                    elif what == "hi":
                        split_half(layer, AT_IN + step[1], step[2])
                    elif what == "sq":
                        act.wait_ge(act_out.sem, act_out.at(t, layer))
                        if t >= 2:
                            act.wait_ge(sq_summed.sem, sq_summed.at(t - 2, layer))
                        act.activation(SQX[t % 2][:, :], QKV[:, t, :], ACT.Square).then_inc(qk_sq.sem, 1)
                    elif what == "gate_cols":
                        act.wait_ge(to_act.sem, to_act.at(0, layer))
                        act.activation(T0, B8[:, :, 0:HEADS], ACT.Exp, scale=-1.0)
                        ch.step(act.activation(T2, T1, ACT.Exp, scale=-1.0))
                        act.activation(T3, T2, ACT.Ln, bias=1.0).then_inc(to_dve.sem, 1)
                    elif what == "cum":
                        act.wait_ge(filled.sem, filled.at(GROUP_INDEX[step], layer))
                        act.wait_ge(to_act.sem, to_act.at(1, layer))
                        act.activation(EG, GCOL, ACT.Exp)
                        act.activation(KTS, T2, ACT.Exp)
                        act.activation(EL, GLAST, ACT.Exp)
                        evacuated(act.activation(SEQ_EL[:, :, :], SEQ_GL, ACT.Exp))
                    elif what == "key_norms":
                        act.wait_ge(to_act.sem, to_act.at(2, layer))
                        act.activation(NK, SSQ[:, :, HEADS:], ACT.Sqrt).then_inc(key_norm.sem, 1)
                    elif what == "gb":
                        act.wait_ge(dd_raw.sem, dd_raw.at(NTH[step], layer))
                        act.activation(DA[:, t, :, :], DA[:, t, :, :], ACT.Exp).then_inc(dd_exp.sem, 1)
                        evacuated(act.activation(QKM[:, t, :, :], heads_bank(step), ACT.Exp))
                    elif what == "nt":
                        evacuated(act.activation(NI[:, t, :, :], group(step, layer), ACT.Copy))
                    elif what == "vt":
                        act.wait_ge(key_norm.sem, key_norm.at(0, layer))
                        scaled_copy(VS[:, t, :, :], step, layer, NK[:, t, :])
                    elif what == "kt":
                        act.wait_ge(evac["act"].sem, evac["act"].at(LEFT_PSUM["cum",][1], layer))
                        scaled_copy(KTL[:, t, :, :], step, layer, KTS[:, t, :])
                    elif what == "ksT" and t == HEADS - 1:
                        act.wait_ge(seq_read.sem, seq_read.at(0, layer))
                        act.wait_ge(kst_zero.sem, kst_zero.at(0, layer))
                        act.activation(KST[:, :, 0:N_SAMPLE], SEQ_READ[:, :, 0:N_SAMPLE], ACT.Copy).then_inc(seq_keys.sem, 1)
                    elif what == "o" and t == C_TILE:
                        act.wait_ge(seq_out.sem, seq_out.at(0, layer))
                        act.activation(kT(tcols(t)), SEQ_READ, ACT.Copy)
                        act.activation(vT(tcols(t)), SEQ_READ, ACT.Square).then_inc(seq_copied.sem, 1)
                    elif what == "o":
                        act.activation(kT(tcols(t)), group(step, layer), ACT.Copy)
                        evacuated(act.activation(vT(tcols(t)), heads_bank(step), ACT.Square))
                    elif what == "o_cols":
                        act.wait_ge(to_act.sem, to_act.at(3 + NTH[step], layer))
                        act.activation(T1[:, t, :], T0[:, t, :], ACT.Sqrt).then_inc(to_dve.sem, 1)
                    elif what == "rob":
                        act.wait_ge(o_full.sem, o_full.at(NTH[step], layer))
                        cols = slice(t * P, min((t + 1) * P, T))
                        act.activation(OH[:, :, cols], kT(cols), ACT.Copy).then_inc(o_hi.sem, 1)
                    elif what == "finish":
                        tap0_of(layer, 2 * N_IN - 1)
                        split_half(layer, AT_OUT - 1, 0)
                        split_half(layer, AT_OUT - 1, 1)
                        act.wait_ge(mix_y.sem, mix_y.at(3, layer))
                        act.wait_ge(products.sem, products.at(PR_IN + 2 * N_IN - 1, layer))
                        act.activation(XH[:, HEADS:KT, 0:T], BY[:, :, :], ACT.Copy).then_inc(mix_hi.sem, 1)
                    elif what == "out":
                        m = t
                        out_squares(layer, 1, m, m % 2, T, y_acc.at(KT + m - 2, layer) if m >= 2 else None)
                        if m % 2:
                            split_after(layer, AT_OUT + m // 2)

            act.wait_ge(eps_set, 1)
            for slot in range(2):
                split_high(slot, A_LEN, raw_value(0, slot))
            for m in range(KT):
                prenorm(0, 0, m)
            act.wait_ge(in_gate, 16)
            act.activation(NEG_A[:, :, :], GATE_P[:, :, 0, :], ACT.Exp).then_inc(gate_exp, 1)
            x_norm(0, 0)
            for layer in range(DEPTH):
                ffn(layer, 0)
                act.wait_ge(w8_in.sem, w8_in.at(0, layer))
                if layer > 0:
                    act.wait_ge(small.sem, small.at(0, layer - 1))
                act.activation(W8H[:, :], W8R[:, :], ACT.Copy).then_inc(w8_hi.sem, 1)
                boundary(layer, 0)
                mixer(layer)
                boundary(layer, 1)
                act.wait_ge(new_hist.sem, new_hist.at(1, layer))
                ffn(layer, 1)
                boundary(layer, 2)

        @block.vector
        def _(dve):
            ch = Chain(dve, chain_dve)

            def split_low(slot, length, high):
                dve.wait_ge(split_hi.sem, high)
                dve.tensor_tensor(WL[slot][:, 0:length], RAW[slot][:, 0:length], WH[slot][:, 0:length].bitcast(F32),
                                  ALU.subtract).then_inc(split_lo.sem, 1)

            def split_after(layer, c):
                nxt, at = (layer, c + 2) if c + 2 < CHUNKS else (layer + 1, c + 2 - CHUNKS)
                if nxt < DEPTH:
                    split_low(c % 2, chunk_length(at), split_hi.at(at, nxt))

            def prenorm(layer, j, m):
                dve.wait_ge(x_hi.sem, x_hi.at(j * KT + m, layer))
                dve.scalar_tensor_tensor(XL[:, m, 0:T], X[:, m, :], gain(layer, j, 0, m), XH[:, m, 0:T].bitcast(F32),
                                         ALU.mult, ALU.subtract).then_inc(x_lo.sem, 1)
            def x_norm(layer, j):
                dve.wait_ge(x_root.sem, x_root.at(j, layer))
                dve.reciprocal(RC[:, 3, :], RC[:, 2, :]).then_inc(x_inv.sem, 1)
                dve.wait_ge(x_rows.sem, x_rows.at(j, layer))
                dve.tensor_copy(RB[:, :], X_ROWS).then_inc(x_rb.sem, 1)
                dve.wait_ge(x_rb.sem, x_rb.at(j, layer))

            def out_tile(layer, j, m, b, n, done, ps, before):
                dve.wait_ge(products.sem, done)
                dve.tensor_copy(hidden(Y, m, n), ps[:, 0:n]).then_inc(y_copied.sem, 1)
                dve.wait_ge(y_sq.sem, y_sq.at(j * KT + m, layer))
                if before is None:
                    ins = dve.tensor_copy(ACCY[:, 0:n], SQY[b][:, 0:n])
                else:
                    dve.wait_ge(y_acc.sem, before)
                    ins = dve.tensor_tensor(ACCY[:, 0:n], ACCY[:, 0:n], SQY[b][:, 0:n], ALU.add)
                ins.then_inc(y_acc.sem, 1)

            def boundary(layer, j):
                n = tokens(2 * layer + 1) if j == 2 else T
                nxt = (layer, j + 1) if j < 2 else (layer + 1, 0)
                dve.wait_ge(y_root.sem, y_root.at(j, layer))
                dve.reciprocal(RC[:, 1, :], RC[:, 0, :]).then_inc(y_inv.sem, 1)
                dve.wait_ge(y_rows.sem, y_rows.at(j, layer))
                for m in range(KT):
                    tmp = TMP[m % 2][:, 0:n]
                    if m >= 2:
                        dve.wait_ge(x_new.sem, x_new.at(j * KT + m - 2, layer))
                    ch.step(dve.scalar_tensor_tensor(tmp, Y[:, m, 0:n], gain(layer, j, 1, m), Y_ROWS[:, 0:n],
                                                     ALU.mult, ALU.mult))
                    dve.tensor_tensor(X[:, m, 0:n], X[:, m, 0:n], tmp, ALU.add).then_inc(x_new.sem, 1)
                    if m > 0 and nxt[0] < DEPTH:
                        prenorm(*nxt, m - 1)
                if nxt[0] < DEPTH:
                    prenorm(*nxt, KT - 1)
                    x_norm(*nxt)

            def ffn(layer, s):
                j, n = 2 * s, tokens(2 * layer + s)

                def up_tile(c, k, split):
                    dve.wait_ge(products.sem, products.at(PR_UP[s] + c, layer))
                    dve.tensor_tensor(GR[k][:, 0:n], PS[:, 2 * k, 0:n], RB[:, 0:n], ALU.mult).then_inc(gate_scaled.sem, 1)
                    dve.tensor_tensor(UR[k][:, 0:n], PS[:, 2 * k + 1, 0:n], RB[:, 0:n], ALU.mult).then_inc(up_scaled.sem, 1)
                    split()
                    dve.wait_ge(silu_done.sem, silu_done.at(s * FT + c, layer))
                    dve.wait_ge(up_scaled.sem, up_scaled.at(s * FT + c, layer))
                    dve.tensor_tensor(HF[k][:, 0:n], SG[k][:, 0:n], UR[k][:, 0:n], ALU.mult).then_inc(h_full.sem, 1)
                    dve.wait_ge(h_hi.sem, h_hi.at(s * FT + c, layer))
                    dve.tensor_tensor(hidden(HL, c, n), HF[k][:, 0:n], hidden(HH, c, n).bitcast(F32),
                                      ALU.subtract).then_inc(h_lo.sem, 1)

                with dve.Fori(0, N_UP // 2 - 1) as i:
                    for k in range(2):
                        up_tile(2 * i + k, k, lambda: split_low(k, A_LEN, split_hi.at(AT_UP[s] + 2 * i + k + 2, layer)))
                for k in range(2):
                    c = N_UP - 2 + k
                    up_tile(c, k, lambda: split_after(layer, AT_UP[s] + c))

                def out(m, b, old):
                    out_tile(layer, j, m, b, n, products.at(PR_DOWN[s] + 2 * m + 1, layer), PS[:, 2 * b, :],
                             y_acc.at(j * KT + m - 1, layer) if old else None)

                for b in range(2):
                    for k in range(2):
                        split_after(layer, AT_DOWN[s] + 2 * b + k)
                    out(b, b, b > 0)
                with dve.Fori(1, KT // 2 - 1) as i:
                    for b in range(2):
                        for k in range(2):
                            split_low(k, D_LEN, split_hi.at(AT_DOWN[s] + 4 * i + 2 * b + k + 2, layer))
                        out(2 * i + b, b, True)
                for b in range(2):
                    m = KT - 2 + b
                    if b == 0:
                        for k in range(2):
                            split_after(layer, AT_DOWN[s] + 2 * m + k)
                    out(m, b, True)
                    if b == 1:
                        for k in range(2):
                            split_after(layer, AT_DOWN[s] + 2 * m + k)

            def convolve(layer, i):
                kind, n = PROJ[i]
                if kind not in ("qkv", "h"):
                    return
                at, taps, steps, src, length = ((C_CG, GW, QKV_T, EXT, G_LEN) if kind == "qkv"
                                                else (C_CS, SW, 4, UEXT, S_LEN))
                k = n % 2
                cv = CV[k][:, 0:length - taps + 1]
                dve.wait_ge(tap0.sem, tap0.at(n + (QKV_T if kind == "h" else 0), layer))
                for tap in range(1, taps):
                    col = at + tap * steps + n
                    ins = dve.scalar_tensor_tensor(cv, src[:, n, tap:tap + length - taps + 1],
                                                   PAR_ALL[:, layer, col:col + 1], cv, ALU.mult, ALU.add)
                    if tap < taps - 1 or kind == "h":
                        ch.step(ins)
                    else:
                        ins.then_inc(conv_done.sem, 1)
                if kind == "h":
                    by = BY[:, n, :]
                    dve.tensor_tensor(by[:, 0:N_PROMPT], by[:, 0:N_PROMPT], CV[k][:, N_META:N_META + N_PROMPT], ALU.mult)
                    dve.tensor_tensor(by[:, N_PROMPT + N_SAMPLE:T], by[:, N_PROMPT + N_SAMPLE:T], CV[k][:, 0:N_META],
                                      ALU.mult)
                    dve.tensor_tensor(seqs(by[:, N_PROMPT:N_PROMPT + N_SAMPLE]), seqs(by[:, N_PROMPT:N_PROMPT + N_SAMPLE]),
                                      seqs(CV[k][:, S_SEQ0:S_SEQ0 + SEQS * S_STEP])[:, :, 0:SEQ_T],
                                      ALU.mult).then_inc(mix_y.sem, 1)

            def spread(dst, hist, seq0, step, ps, by):
                dve.tensor_tensor(dst[:, hist:hist + N_META], ps[:, N_PROMPT + N_SAMPLE:T],
                                  by[:, N_PROMPT + N_SAMPLE:T], ALU.mult)
                dve.tensor_tensor(dst[:, hist + N_META:seq0], ps[:, 0:N_PROMPT], by[:, 0:N_PROMPT], ALU.mult)
                return dve.tensor_tensor(seqs(dst[:, seq0:])[:, :, hist:], seqs(ps[:, N_PROMPT:N_PROMPT + N_SAMPLE]),
                                         seqs(by[:, N_PROMPT:N_PROMPT + N_SAMPLE]), ALU.mult)

            def split_half(layer, c):
                cols = slice(0, A_LEN // 2)
                dve.wait_ge(split_hi.sem, split_hi.at(c + 2, layer))
                dve.tensor_tensor(WL[c % 2][:, cols], RAW[c % 2][:, cols], WH[c % 2][:, cols].bitcast(F32),
                                  ALU.subtract).then_inc(split_lo.sem, 1)

            def projected(layer, i):
                kind, n = PROJ[i]
                ps = PS[:, proj_bank(i), :]
                dve.wait_ge(products.sem, products.at(PR_IN + i, layer))
                if kind == "qkv":
                    dve.wait_ge(hist_set.sem, hist_set.at(0, layer))
                    ins = spread(EXT[:, n, :], G_HIST, G_SEQ0, G_STEP, ps, RB)
                elif kind == "z":
                    ins = dve.tensor_tensor(ZS[:, n, :], ps[:, 0:T], RB[:, :], ALU.mult)
                elif kind == "b":
                    ins = dve.tensor_tensor(BY[:, n, :], ps[:, 0:T], RB[:, :], ALU.mult)
                elif kind == "c":
                    ins = dve.tensor_tensor(TMP[n % 2][:, :], ps[:, 0:T], RB2[:, :], ALU.mult)
                else:
                    dve.wait_ge(proj_read.sem, proj_read.at(i - 1, layer))
                    ins = spread(UEXT[:, n, :], S_HIST, S_SEQ0, S_STEP, ps, TMP[n % 2])
                ins.then_inc(proj_read.sem, 1)

            def group(name, layer):
                dve.wait_ge(filled.sem, filled.at(GROUP_INDEX[name], layer))
                return heads_bank(name)

            def evacuated(ins):
                ins.then_inc(evac["dve"].sem, 1)

            def own(name, layer):
                dve.wait_ge(evac["dve"].sem, evac["dve"].at(LEFT_PSUM[name][1], layer))

            def act_group(name, layer):
                dve.wait_ge(evac["act"].sem, evac["act"].at(LEFT_PSUM[name][1], layer))

            def mixer(layer):
                for step in STEPS:
                    what, t = step[0], step[-1]
                    if what == "evac":
                        projected(layer, t)
                    elif what == "conv":
                        convolve(layer, t)
                    elif what == "lo":
                        split_half(layer, AT_IN + t)
                    elif what == "sq_rows" and t == 2 * HEADS - 1:
                        dve.wait_ge(sq_summed.sem, sq_summed.at(t, layer))
                        dve.wait_ge(small.sem, small.at(0, layer))
                        dve.tensor_copy(ACCX[0:2 * HEADS, 0:T], SQ_ROWS).then_inc(sq_out.sem, 1)
                    elif what == "gate_rows":
                        dve.wait_ge(filled.sem, filled.at(GROUP_INDEX[step], layer))
                        evacuated(dve.tensor_tensor(ACCX[0:2 * HEADS, 0:T], GATE_ROWS, RB[0:2 * HEADS, :], ALU.mult))
                    elif what == "gate_cols":
                        dve.wait_ge(small.sem, small.at(0, layer))
                        ch.step(dve.tensor_copy(B8[:, :, :], P8))
                        dt_bias = GATE_P[:, layer, 1, :].unsqueeze(1).to_broadcast([P, TT, HEADS])
                        ch.step(dve.tensor_tensor(T4, B8[:, :, HEADS:], dt_bias, ALU.add))
                        dve.scalar_tensor_tensor(T1, T4, -1.0, T4, ALU.mult, ALU.max).then_inc(to_act.sem, 1)
                    elif what == "gate_g":
                        dve.wait_ge(to_dve.sem, to_dve.at(0, layer))
                        ch.step(dve.tensor_scalar(T0, T0, 1.0, None, ALU.add))
                        dve.reciprocal(BETA, T0)
                        ch.step(dve.scalar_tensor_tensor(T3, T4, 0.0, T3, ALU.max, ALU.add))
                        neg_a = NEG_A[:, layer, :].unsqueeze(1).to_broadcast([P, TT, HEADS])
                        ch.step(dve.scalar_tensor_tensor(G, T3, -1.0, neg_a, ALU.mult, ALU.mult))
                        shape = [P, HEADS, SEQS + 1]
                        dve.tensor_tensor(SEQ_G, G[:, C_TILE, :].unsqueeze(2).to_broadcast(shape),
                                          IND[:, :].unsqueeze(1).to_broadcast(shape), ALU.mult).then_inc(gate_g.sem, 1)
                    elif what == "cum":
                        dve.wait_ge(filled.sem, filled.at(GROUP_INDEX[step], layer))
                        ch.step(dve.tensor_copy(GC, GCOL))
                        dve.tensor_tensor(T2, GLAST, GC, ALU.subtract).then_inc(to_act.sem, 1)
                    elif what == "norms":
                        ch.step(dve.tensor_tensor(RB2[:, :], RB[:, :], RB[:, :], ALU.mult))
                        act_group(("cum",), layer)
                        ch.step(dve.tensor_scalar(NEG_EG, EG, -1.0, None, ALU.mult))
                        dve.wait_ge(qk_cols.sem, qk_cols.at(0, layer))
                        ch.step(dve.tensor_scalar(SSQ[:, :, :], QK_COLS, EPS, None, ALU.add))
                        dve.reciprocal(T0, SSQ[:, :, HEADS:]).then_inc(to_act.sem, 1)
                        dve.wait_ge(to_act.sem, to_act.at(2, layer))
                        dve.tensor_tensor(CK, T0, BETA, ALU.mult)
                        ch.step(dve.tensor_scalar(WQ, SSQ[:, :, 0:HEADS], EPS * P, None, ALU.mult))
                    elif what == "gb":
                        gb = group(step, layer)
                        for h in range(HEADS):
                            ins = dve.tensor_scalar(DA[:, t, h, :], gb[:, h, :], GC[:, t, h:h + 1], 0.0, ALU.subtract, ALU.min)
                        ins.then_inc(dd_raw.sem, 1)
                    elif what == "qk":
                        group(step, layer)
                        act_group(("gb", t), layer)
                        dve.tensor_tensor(qT(tcols(t)), qT(tcols(t)), QKM[:, t, :, :], ALU.mult).then_inc(q_decayed.sem, 1)
                        dve.wait_ge(q_decayed.sem, q_decayed.at(NTH[step], layer))
                        dve.wait_ge(dd_exp.sem, dd_exp.at(NTH[step], layer))
                        evacuated(dve.tensor_tensor(QKM[:, t, :, :], group(step, layer), DA[:, t, :, :], ALU.mult))
                    elif what == "kk":
                        own(("qk", t), layer)
                        kk = group(step, layer)
                        for h in range(HEADS):
                            ins = dve.scalar_tensor_tensor(DA[:, t, h, :], kk[:, h, :], CK[:, t, h:h + 1], DA[:, t, h, :],
                                                           ALU.mult, ALU.mult)
                        evacuated(ins)
                    elif what == "pair":
                        own(("kk", t), layer)
                        if NTH[step] == 0:
                            dve.wait_ge(new_hist.sem, new_hist.at(0, layer))
                            dve.wait_ge(conv_done.sem, conv_done.at(QKV_T - 1, layer))
                        ch.step(dve.tensor_tensor(MI[:, t, :, :], DA[:, t, :, :], heads_of(mask("pair")), ALU.mult))
                        dve.tensor_tensor(MI[:, t, :, :], heads_of(mask("ident")), MI[:, t, :, :],
                                          ALU.subtract).then_inc(pair_set.sem, 1)
                    elif what == "x":
                        _, t, m = step
                        group(step, layer)
                        name = "lv8_meta" if t == C_TILE and m == 8 else f"lv{m}"
                        evacuated(dve.tensor_tensor(XB[t], heads_bank(step), heads_of(mask(name)), ALU.mult))
                    elif what == "y":
                        _, t, m = step
                        even = blocks(NI[:, t, :, :], m, 0)
                        evacuated(dve.tensor_tensor(even, even, blocks(group(step, layer), m, 0), ALU.subtract))
                    elif what == "yt":
                        _, t, m = step
                        odd = blocks(MI[:, t, :, :], m, 1)
                        evacuated(dve.tensor_tensor(odd, odd, blocks(group(step, layer), m, 1), ALU.subtract))
                    elif what in ("kst", "ks"):
                        t = C_TILE if what == "kst" else t
                        act_group(("vt", t), layer)
                        ks = group(step, layer)
                        for h in range(HEADS):
                            ins = dve.scalar_tensor_tensor(VS[:, t, h, :], ks[:, h, :], NEG_EG[:, t, h:h + 1], VS[:, t, h, :],
                                                           ALU.mult, ALU.add)
                        evacuated(ins)
                    elif what == "nv":
                        evacuated(dve.tensor_tensor(NVP[:, t, :, :], group(step, layer), per_head(CK[:, t, :]), ALU.mult))
                    elif what == "st":
                        st = group(step, layer)
                        if t == C_TILE:
                            if layer > 0:
                                dve.wait_ge(states_out.sem, states_out.at(1, layer - 1))
                            ins = dve.tensor_copy(PR_S[:, :, :], st)
                        else:
                            for h in range(HEADS):
                                ins = dve.scalar_tensor_tensor(PR_S[:, h, :], PR_S[:, h, :], EL[:, t, h:h + 1], st[:, h, :],
                                                               ALU.mult, ALU.add)
                        evacuated(ins)
                    elif what == "spread":
                        _, h, half = step
                        buf = SEQ_BUF[NTH[step] % 2]
                        per_seq = NVP[0:N_SAMPLE, C_TILE, h, :].unsqueeze(1).to_broadcast([N_SAMPLE, 4, P])
                        which = IND[0:N_SAMPLE, 4 * half:4 * half + 4].unsqueeze(2).to_broadcast([N_SAMPLE, 4, P])
                        own(("nv", C_TILE), layer)
                        if NTH[step] >= 2:
                            dve.wait_ge(filled.sem, filled.at(GROUP_INDEX[SEQ_NAMES[NTH[step] - 2]], layer))
                        dve.tensor_tensor(buf[0:N_SAMPLE, :, :], per_seq, which, ALU.mult).then_inc(seq_spread.sem, 1)
                    elif what == "sn":
                        _, h, half = step
                        sn = group(step, layer)
                        for q in range(4):
                            s = 4 * half + q
                            ins = dve.scalar_tensor_tensor(SEQ_S[:, s, h, :], SEQ_S[:, s, h, :], SEQ_EL[:, h, s:s + 1],
                                                           sn[:, q, :], ALU.mult, ALU.add)
                        evacuated(ins)
                    elif what == "o_cols":
                        dve.wait_ge(small.sem, small.at(1 + NTH[step], layer))
                        dve.scalar_tensor_tensor(T0[:, t, :], O_COLS[:, t, :], 1.0 / P, WQ[:, t, :],
                                                 ALU.mult, ALU.add).then_inc(to_act.sem, 1)
                    elif what == "o_inv":
                        dve.wait_ge(to_dve.sem, to_dve.at(1 + NTH[step], layer))
                        dve.reciprocal(RO[:, t, :], T1[:, t, :]).then_inc(o_inv.sem, 1)
                    elif what == "rob":
                        cols = slice(t * P, min((t + 1) * P, T))
                        n = cols.stop - cols.start
                        if t == C_TILE:
                            dve.wait_ge(seq_copied.sem, seq_copied.at(0, layer))
                        else:
                            act_group(("o", t), layer)
                        rob = group(step, layer)
                        ins = dve.scalar_tensor_tensor(kT(cols), kT(cols), PAR_ALL[:, layer, C_GN:C_GN + 1], rob[:, :, 0:n],
                                                       ALU.mult, ALU.mult)
                        evacuated(ins)
                        own(step, layer)
                        dve.wait_ge(act_out.sem, act_out.at(QKV_T + 3, layer))
                        dve.tensor_tensor(kT(cols), kT(cols), ZS[:, :, cols], ALU.mult).then_inc(o_full.sem, 1)
                    elif what == "o_low":
                        cols = slice(t * P, min((t + 1) * P, T))
                        dve.wait_ge(o_hi.sem, o_hi.at(NTH[step], layer))
                        dve.tensor_tensor(OL[:, :, cols], kT(cols), OH[:, :, cols].bitcast(F32),
                                          ALU.subtract).then_inc(o_lo.sem, 1)
                    elif what == "finish":
                        convolve(layer, 2 * N_IN - 1)
                        split_half(layer, AT_OUT - 1)
                        dve.wait_ge(mix_hi.sem, mix_hi.at(0, layer))
                        dve.tensor_tensor(XL[:, HEADS:KT, 0:T], BY[:, :, :], XH[:, HEADS:KT, 0:T].bitcast(F32),
                                          ALU.subtract).then_inc(mix_lo.sem, 1)
                    elif what == "out":
                        m = t
                        out_tile(layer, 1, m, m % 2, T, products.at(PR_OUT + m, layer), PS[:, m % 4, :],
                                 y_acc.at(KT + m - 1, layer) if m else None)
                        if m % 2:
                            split_after(layer, AT_OUT + m // 2)

            dve.memset(EPSC[:, :], EPS).then_inc(eps_set, 1)
            dve.wait_ge(in_par, 16)
            for layer in range(DEPTH):
                for s in range(2):
                    at = C_GAIN + KT * (4 * s + 1)
                    ch.step(dve.tensor_scalar(HALF_G[:, layer, s, :], PAR_ALL[:, layer, at:at + KT], 0.5, None, ALU.mult))
            for slot in range(2):
                split_low(slot, A_LEN, split_hi.at(slot))
            for m in range(KT):
                if m == 0:
                    dve.wait_ge(zeroed, 1)
                prenorm(0, 0, m)
            x_norm(0, 0)
            dve.wait_ge(gate_exp, 1)
            for layer in range(DEPTH):
                ffn(layer, 0)
                dve.wait_ge(w8_hi.sem, w8_hi.at(0, layer))
                dve.tensor_tensor(W8L[:, :], W8R[:, :], W8H[:, :].bitcast(F32), ALU.subtract).then_inc(w8_lo.sem, 1)
                boundary(layer, 0)
                mixer(layer)
                boundary(layer, 1)
                dve.wait_ge(new_hist.sem, new_hist.at(1, layer))
                ffn(layer, 1)
                boundary(layer, 2)

        @block.tensor
        def _(pe):
            def three(out, wh, wl, xh, xl, first, last):
                pe.matmul(out, wh, xh, start=first, stop=False)
                pe.matmul(out, wh, xl, start=False, stop=False)
                return pe.matmul(out, wl, xh, start=False, stop=last)

            def block_of(slot, at):
                return WH[slot][:, at * P:(at + 1) * P], WL[slot][:, at * P:(at + 1) * P]

            def x_tile(kt, n):
                return XH[:, kt, 0:n], XL[:, kt, 0:n]

            def columns(acc, out, ready):
                pe.wait_ge(ready[0], ready[1])
                for t in range(TT):
                    ins = pe.matmul(out[:, t:t + 1], acc[:, tcols(t)], mask("ones", 1), start=True, stop=True)
                return ins

            def rows(col, out):
                for t in range(TT):
                    n = min(P, T - t * P)
                    ins = pe.matmul(out[:, t * P:t * P + n], col[:, t:t + 1].to_broadcast([P, P]), mask("ident", n),
                                    start=True, stop=True)
                return ins

            def entry(layer, j, at, n, first_product):
                for slot in range(2):
                    pe.wait_ge(split_lo.sem, split_lo.at(at + slot, layer))
                early = 5

                def part(slot, kt):
                    for half in range(2):
                        ins = three(PS[:, 2 * slot + half, 0:n], *block_of(slot, half * KT + kt), *x_tile(kt, n),
                                    kt == 0, kt == KT - 1)
                        if kt == KT - 1 and (half == 1 or first_product):
                            ins.then_inc(products.sem, 1)

                def ready(kt):
                    pe.wait_ge(x_lo.sem, x_lo.at(j * KT + kt, layer))

                for kt in range(early):
                    ready(kt)
                    part(0, kt)
                    part(1, kt)
                for kt in range(early, KT):
                    ready(kt)
                    part(0, kt)
                if (layer, j) == (0, 0):
                    pe.wait_ge(in_masks, 32)
                part(1, early)
                columns(ACCX, X_COLS, (x_acc.sem, x_acc.at(j * KT + KT - 1, layer))).then_inc(x_cols.sem, 1)
                part(1, early + 1)
                pe.wait_ge(x_inv.sem, x_inv.at(j, layer))
                rows(RC[:, 3, :], X_ROWS).then_inc(x_rows.sem, 1)
                for kt in range(early + 2, KT):
                    part(1, kt)

            def ffn(layer, s):
                j, n = 2 * s, tokens(2 * layer + s)
                entry(layer, j, AT_UP[s], n, False)

                def up_chunk(i, k):
                    c = 2 * i + k
                    pe.wait_ge(split_lo.sem, split_lo.at(AT_UP[s] + c, layer))
                    pe.wait_ge(up_scaled.sem, up_scaled.at(s * FT + c - 2, layer))
                    for half in range(2):
                        for kt in range(KT):
                            ins = three(PS[:, 2 * k + half, 0:n], *block_of(k, half * KT + kt), *x_tile(kt, n),
                                        kt == 0, kt == KT - 1)
                    ins.then_inc(products.sem, 1)

                with pe.Fori(1, N_UP // 2) as i:
                    for k in range(2):
                        up_chunk(i, k)

                def down_tile(m, b, first=False, old=True):
                    for half in range(2):
                        pe.wait_ge(split_lo.sem, split_lo.at(AT_DOWN[s] + 2 * m + half, layer))
                        if half == 0 and old:
                            pe.wait_ge(y_copied.sem, y_copied.at(j * KT + m - 2, layer))
                        if half == 0 and not old:
                            pe.wait_ge(gate_scaled.sem, gate_scaled.at(s * FT + FT - 2 + b, layer))
                        for q in range(DH):
                            f = half * DH + q
                            if first:
                                pe.wait_ge(h_lo.sem, h_lo.at(s * FT + f, layer))
                            ins = three(PS[:, 2 * b, 0:n], *block_of(half, q), HH[:, f, 0:n], HL[:, f, 0:n],
                                        f == 0, f == FT - 1)
                        ins.then_inc(products.sem, 1)

                down_tile(0, 0, first=True, old=False)
                down_tile(1, 1, old=False)
                with pe.Fori(1, KT // 2) as i:
                    for b in range(2):
                        down_tile(2 * i + b, b)

            def out_norm(layer, j):
                columns(ACCY, Y_COLS, (y_acc.sem, y_acc.at(j * KT + KT - 1, layer))).then_inc(y_cols.sem, 1)
                pe.wait_ge(y_inv.sem, y_inv.at(j, layer))
                rows(RC[:, 1, :], Y_ROWS).then_inc(y_rows.sem, 1)

            def evacuated(name, layer):
                engine, count = LEFT_PSUM[name]
                pe.wait_ge(evac[engine].sem, evac[engine].at(count, layer))

            def bank_free(name, layer):
                index = GROUP_INDEX[name]
                if index >= 3:
                    evacuated(GROUP_ORDER[index - 3], layer)

            def per_head_products(name, layer, lhsT, rhs, transpose=False):
                bank_free(name, layer)
                out = heads_bank(name)
                for h in range(HEADS):
                    if transpose:
                        ins = pe.transpose(out[:, h, :], lhsT(h), mask("ident"))
                    else:
                        ins = pe.matmul(out[:, h, :], lhsT(h), rhs(h), start=True, stop=True)
                ins.then_inc(filled.sem, 1)

            def o_half(m, first, last):
                for kt in range(HEADS):
                    three(PS[:, m % 4, 0:T], *block_of((m // 2) % 2, (m % 2) * KT + kt), OH[:, kt, 0:T], OL[:, kt, 0:T],
                          first and kt == 0, last and kt == HEADS - 1)

            def mixer(layer):
                for step in STEPS:
                    what, t = step[0], step[-1]
                    if what == "entry":
                        entry(layer, 1, AT_IN, T, True)
                    elif what == "part":
                        _, i, part = step
                        first, end = PART_KT[part]
                        slot = (i // 2) % 2
                        if part == 0:
                            pe.wait_ge(proj_read.sem, proj_read.at(i - 4 if i < 7 else i - 3, layer))
                            pe.wait_ge(split_lo.sem, split_lo.at(AT_IN + i // 2, layer))
                            pe.wait_ge(split_lo2.sem, split_lo2.at(i // 2 - 2, layer))
                        for kt in range(first, end):
                            ins = three(PS[:, proj_bank(i), 0:T], *block_of(slot, (i % 2) * KT + kt), *x_tile(kt, T),
                                        kt == 0, kt == KT - 1)
                        if end == KT:
                            ins.then_inc(products.sem, 1)
                    elif what == "sq_rows":
                        pe.wait_ge(qk_sq.sem, qk_sq.at(t, layer))
                        if t == 0:
                            pe.wait_ge(to_act.sem, to_act.at(0, layer))
                        pick = MK[:, MASKS.index("pick"), PICK_AT - t:PICK_AT - t + 2 * HEADS]
                        pe.matmul(SQ_ROWS, pick, SQX[t % 2][:, 0:T], start=(t == 0),
                                  stop=(t == 2 * HEADS - 1)).then_inc(sq_summed.sem, 1)
                    elif what == "sq_cols":
                        pe.wait_ge(sq_out.sem, sq_out.at(0, layer))
                        for q in range(TT):
                            ins = pe.transpose(QK_COLS[:, q, :], ACCX[0:2 * HEADS, tcols(q)], mask("ident", 2 * HEADS)[0:2 * HEADS])
                        ins.then_inc(qk_cols.sem, 1)
                    elif what == "gate_rows":
                        pe.wait_ge(w8_lo.sem, w8_lo.at(0, layer))
                        for kt in range(KT):
                            cols = slice(2 * HEADS * kt, 2 * HEADS * (kt + 1))
                            ins = three(GATE_ROWS, W8H[:, cols], W8L[:, cols], *x_tile(kt, T), kt == 0, kt == KT - 1)
                        ins.then_inc(filled.sem, 1)
                    elif what == "gate_cols":
                        evacuated(("gate_rows",), layer)
                        for q in range(TT):
                            ins = pe.transpose(P8[:, q, :], ACCX[0:2 * HEADS, tcols(q)], mask("ident", 2 * HEADS)[0:2 * HEADS])
                        ins.then_inc(small.sem, 1)
                    elif what == "cum":
                        pe.wait_ge(gate_g.sem, gate_g.at(0, layer))
                        bank_free(step, layer)
                        pe.matmul(GCOL[:, C_TILE, :], incl(C_TILE), G[:, C_TILE, :], start=True, stop=True)
                        pe.matmul(GLAST[:, C_TILE, :], mask("same_seq"), G[:, C_TILE, :], start=True, stop=True)
                        pe.matmul(GCOL[:, 0:C_TILE, :], incl(0), G[:, 0:C_TILE, :], start=True, stop=True)
                        pe.matmul(GLAST[:, 0:C_TILE, :], mask("ones"), G[:, 0:C_TILE, :], start=True, stop=True)
                        ins = pe.matmul(SEQ_GL, mask("ones"), SEQ_G, start=True, stop=True)
                        ins.then_inc(filled.sem, 1)
                    elif what == "gb":
                        per_head_products(step, layer, lambda h: G[:, t, h:h + 1].to_broadcast([P, P]),
                                          lambda h: incl(t))
                    elif what == "qk":
                        pe.wait_ge(act_out.sem, act_out.at(2 * HEADS - 1, layer))
                        per_head_products(step, layer, lambda h: kT(tcols(t))[:, h, :], lambda h: qT(tcols(t))[:, h, :])
                    elif what == "kk":
                        per_head_products(step, layer, lambda h: kT(tcols(t))[:, h, :], lambda h: kT(tcols(t))[:, h, :])
                    elif what == "vt":
                        pe.wait_ge(act_out.sem, act_out.at(QKV_T - 1, layer))
                        per_head_products(step, layer, lambda h: vT(tcols(t))[:, h, :], None, transpose=True)
                    elif what == "nt":
                        pe.wait_ge(pair_set.sem, pair_set.at(NTH["pair", t], layer))
                        per_head_products(step, layer, lambda h: MI[:, t, h, :], None, transpose=True)
                    elif what == "x":
                        _, t, m = step
                        evacuated(("nt", t) if m == 2 else ("yt", t, m // 2), layer)
                        per_head_products(step, layer, lambda h: DA[:, t, h, :], lambda h: NI[:, t, h, :])
                    elif what == "y":
                        evacuated(("x", *step[1:]), layer)
                        t = step[1]
                        per_head_products(step, layer, lambda h: MI[:, t, h, :], lambda h: XB[t][:, h, :])
                    elif what == "yt":
                        evacuated(("x", *step[1:]), layer)
                        t = step[1]
                        per_head_products(step, layer, lambda h: XB[t][:, h, :], lambda h: MI[:, t, h, :])
                    elif what == "kt":
                        per_head_products(step, layer, lambda h: kT(tcols(t))[:, h, :], None, transpose=True)
                    elif what == "ksT":
                        h = t
                        if h == 0:
                            pe.wait_ge(states_in.sem, states_in.at(0, layer))
                            pe.wait_ge(proj_read.sem, proj_read.at(3, layer))
                        for s in range(SEQS):
                            cols = slice(N_PROMPT + s * SEQ_T, N_PROMPT + (s + 1) * SEQ_T)
                            ins = pe.matmul(SEQ_READ[:, h, s * SEQ_T:(s + 1) * SEQ_T], SEQ_S[:, s, h, :], kT(cols)[:, h, :],
                                            start=True, stop=True)
                        if h == HEADS - 1:
                            ins.then_inc(seq_read.sem, 1)
                    elif what == "oC":
                        h, t = t, C_TILE
                        if h == 0:
                            pe.wait_ge(seq_keys.sem, seq_keys.at(0, layer))
                            evacuated(("nv", t), layer)
                            pe.wait_ge(q_decayed.sem, q_decayed.at(ORDER.index(t), layer))
                            pe.wait_ge(qk_masked.sem, qk_masked.at(ORDER.index(t), layer))
                        for s in range(SEQS):
                            cols = slice(N_PROMPT + s * SEQ_T, N_PROMPT + (s + 1) * SEQ_T)
                            pe.matmul(SEQ_READ[:, h, s * SEQ_T:(s + 1) * SEQ_T], SEQ_S[:, s, h, :], qT(cols)[:, h, :],
                                      start=(s == 0), stop=False)
                        pe.matmul(SEQ_READ[:, h, 0:N_SAMPLE], NVP[:, t, h, :], QKM[:, t, h, 0:N_SAMPLE],
                                  start=False, stop=True)
                        ins = pe.matmul(SEQ_READ[:, h, N_SAMPLE:], NVP[:, t, h, :], QKM[:, t, h, N_SAMPLE:],
                                        start=True, stop=True)
                        if h == HEADS - 1:
                            ins.then_inc(seq_out.sem, 1)
                    elif what == "kst":
                        pe.wait_ge(seq_keys.sem, seq_keys.at(0, layer))
                        per_head_products(step, layer, lambda h: KST[:, h, :], None, transpose=True)
                    elif what == "ks":
                        evacuated(("st", ORDER[ORDER.index(t) - 1]), layer)
                        per_head_products(step, layer, lambda h: kT(tcols(t))[:, h, :], lambda h: PR_S[:, h, :])
                    elif what == "nv":
                        evacuated(("kst",) if t == C_TILE else ("ks", t), layer)
                        evacuated(("yt", t, LEVELS[t][-1]), layer)
                        per_head_products(step, layer, lambda h: MI[:, t, h, :], lambda h: VS[:, t, h, :])
                    elif what == "st":
                        evacuated(("nv", t), layer)
                        evacuated(("kt", t), layer)
                        part = slice(META_AT, META_AT + N_META) if t == C_TILE else slice(0, P)
                        per_head_products(step, layer, lambda h: KTL[part, t, h, :], lambda h: NVP[part, t, h, :])
                    elif what == "o" and t != C_TILE:
                        evacuated(("nv", t), layer)
                        pe.wait_ge(q_decayed.sem, q_decayed.at(ORDER.index(t), layer))
                        pe.wait_ge(qk_masked.sem, qk_masked.at(ORDER.index(t), layer))
                        bank_free(step, layer)
                        out = heads_bank(step)
                        for h in range(HEADS):
                            pe.matmul(out[:, h, :], NVP[:, t, h, :], QKM[:, t, h, :], start=True, stop=False)
                            ins = pe.matmul(out[:, h, :], PR_S[:, h, :], qT(tcols(t))[:, h, :], start=False, stop=True)
                        ins.then_inc(filled.sem, 1)
                    elif what == "sn":
                        _, h, half = step
                        evacuated(("kt", C_TILE), layer)
                        pe.wait_ge(seq_spread.sem, seq_spread.at(NTH[step], layer))
                        bank_free(step, layer)
                        pe.matmul(heads_bank(step), KTL[0:N_SAMPLE, C_TILE, h, :], SEQ_BUF[NTH[step] % 2][0:N_SAMPLE, :, :],
                                  start=True, stop=True).then_inc(filled.sem, 1)
                    elif what == "o_cols":
                        if t == C_TILE:
                            pe.wait_ge(seq_copied.sem, seq_copied.at(0, layer))
                        else:
                            evacuated(("o", t), layer)
                        pe.wait_ge(to_act.sem, to_act.at(2 + NTH[step], layer))
                        for h in range(HEADS):
                            ins = pe.matmul(O_COLS[:, t, h:h + 1], vT(tcols(t))[:, h, :], mask("ones", 1),
                                            start=True, stop=True)
                        ins.then_inc(small.sem, 1)
                    elif what == "rob":
                        pe.wait_ge(o_inv.sem, o_inv.at(NTH["o_inv", t], layer))
                        per_head_products(step, layer, lambda h: RO[:, t, h:h + 1].to_broadcast([P, P]),
                                          lambda h: mask("ident"))
                    elif what == "out_o":
                        m = t
                        if m == 0:
                            pe.wait_ge(o_lo.sem, o_lo.at(TT - 1, layer))
                        pe.wait_ge(split_lo.sem, split_lo.at(AT_OUT + m // 2, layer))
                        pe.wait_ge(split_lo2.sem, split_lo2.at(N_IN - 2 + m // 2, layer))
                        if m < 3:
                            pe.wait_ge(proj_read.sem, proj_read.at(2 * N_IN - 3 + m, layer))
                        else:
                            pe.wait_ge(seq_copied.sem, seq_copied.at(0, layer))
                        o_half(m, True, False)
                    elif what == "out":
                        m = t
                        if m == 0:
                            pe.wait_ge(mix_lo.sem, mix_lo.at(0, layer))
                        if m >= 4:
                            pe.wait_ge(split_lo.sem, split_lo.at(AT_OUT + m // 2, layer))
                            pe.wait_ge(y_copied.sem, y_copied.at(KT + m - 4, layer))
                            o_half(m, True, False)
                        for kt in range(HEADS, KT):
                            ins = three(PS[:, m % 4, 0:T], *block_of((m // 2) % 2, (m % 2) * KT + kt), *x_tile(kt, T),
                                        False, kt == KT - 1)
                        ins.then_inc(products.sem, 1)

            for layer in range(DEPTH):
                ffn(layer, 0)
                out_norm(layer, 0)
                mixer(layer)
                out_norm(layer, 1)
                ffn(layer, 1)
                out_norm(layer, 2)


def constants():
    at = np.arange(P)
    chunk = np.where(at < N_SAMPLE, at // SEQ_T, np.where(at < META_AT + N_META, SEQS, SEQS + 1))
    row, col = at[:, None], at[None, :]
    same = chunk[:, None] == chunk[None, :]
    found = {
        "ident": row == col, "ones": row >= 0, "incl_full": row <= col, "incl_seq": (row <= col) & same,
        "same_seq": same,
        "pair": (row + 1 == col) & (row % 2 == 0),
    }
    for m in (2, 4, 8, 16, 32, 64):
        found[f"lv{m}"] = (row // (2 * m) == col // (2 * m)) & (row // m % 2 == 1) & (col // m % 2 == 0)
    found["pick"] = (col == PICK_AT) & (row >= 0)
    found["lv8_meta"] = found["lv8"] & (row >= META_AT)
    masks = np.stack([np.broadcast_to(found[name], (P, P)) for name in MASKS], axis=1).astype(np.float32)
    ind = (chunk[:, None] == np.arange(SEQS + 1)[None, :]).astype(np.float32)
    return masks, ind


def features_first(a):
    a = a.reshape(*a.shape[:-1], a.shape[-1] // P, P)
    return np.moveaxis(a, -1, 0)


def layout(a):
    L = DEPTH
    x = np.concatenate([a["x_prompt"][0], a["x_sample"].reshape(N_SAMPLE, D_MODEL), a["meta_tokens"]])
    x = np.ascontiguousarray(x.reshape(T, KT, P).transpose(2, 1, 0))

    def in_tiles(w):
        n = w.shape[2] // P
        return w.reshape(L, KT, P, n, P).transpose(0, 3, 2, 1, 4).reshape(L, n, P, KT * P)

    def pairs(w):
        n = w.shape[1] // 2
        return w.reshape(L, n, 2, P, KT * P).transpose(0, 1, 3, 2, 4).reshape(L, n, P, A_LEN)

    up = [pairs(np.stack([in_tiles(a[f"ffn{s}_gate"]), in_tiles(a[f"ffn{s}_up"])], axis=2).reshape(L, 2 * FT, P, KT * P))
          for s in (1, 2)]
    down = [a[f"ffn{s}_down"].reshape(L, 2, DH, P, KT, P).transpose(0, 4, 1, 3, 2, 5).reshape(L, N_DOWN, P, D_LEN)
            for s in (1, 2)]
    w = a["w_in"]
    gates_at = 4 * HEADS * P
    rest = gates_at + 2 * HEADS
    tiles = np.concatenate([in_tiles(w[:, :, 0:gates_at]), in_tiles(w[:, :, rest:])], axis=1)
    order = list(range(QKV_T + 8))
    for i in range(4):
        order += [20 + i, 24 + i]
    w_8 = w[:, :, gates_at:rest].reshape(L, KT, P, 8).transpose(0, 2, 1, 3).reshape(L, P, KT * 8)
    par = np.concatenate([a["norm_gains"].reshape(L, -1, P), a["conv_gdn"].reshape(L, -1, P),
                          a["conv_sc"].reshape(L, -1, P), a["gdn_norm"].reshape(L, 1, P)], axis=1)
    masks, ind = constants()
    hist_g = a["cache_gdn_conv"].reshape(L, SEQS, G_HIST, QKV_T, P).transpose(4, 0, 3, 1, 2)
    hist_s = a["cache_sconv"].reshape(L, SEQS, S_HIST, 4, P).transpose(4, 0, 3, 1, 2)
    return {
        "x": x, "par": par.transpose(2, 0, 1), "hist_g": hist_g, "hist_s": hist_s,
        "gate_p": np.stack([a["a_log"], a["dt_bias"]], axis=1), "masks": masks, "ind": ind,
        "w_up": np.stack(up, axis=1), "w_down": np.stack(down, axis=1), "w_in": pairs(tiles[:, order]),
        "w_8": w_8, "w_out": pairs(in_tiles(a["w_out"])),
        "states": a["state_gdn"].transpose(0, 3, 1, 2, 4),
    }


OUTS = {
    "y": [P, KT, N_PROMPT + N_SAMPLE], "new_g": [DEPTH, P, QKV_T, 1 + SEQS, G_HIST],
    "new_s": [DEPTH, P, 4, 1 + SEQS, S_HIST], "state_p": [DEPTH, P, HEADS, P], "state_s": [DEPTH, P, SEQS, HEADS, P],
}


def kernel(**inputs):
    import concourse.bacc as bacc
    from concourse.bass_utils import run_bass_kernel_spmd

    nc = bacc.Bacc("TRN2", target_bir_lowering=False, num_devices=1)
    arrays, io = {}, {}
    for name, a in layout({k: np.asarray(v) for k, v in inputs.items()}).items():
        arrays[f"in_{name}"] = np.ascontiguousarray(a)
        io[name] = nc.dram_tensor(f"in_{name}", a.shape, F32, kind="ExternalInput").ap()
    for name, shape in OUTS.items():
        io[name] = nc.dram_tensor(f"out_{name}", shape, F32, kind="ExternalOutput").ap()
    decoder_trunk(nc, io)
    out = run_bass_kernel_spmd(nc, [arrays], core_ids=[0]).results[0]
    y = out["out_y"].transpose(2, 1, 0).reshape(-1, D_MODEL)
    new_g = out["out_new_g"].transpose(0, 3, 4, 2, 1).reshape(DEPTH, 1 + SEQS, G_HIST, QKV_T * P)
    new_s = out["out_new_s"].transpose(0, 3, 4, 2, 1).reshape(DEPTH, 1 + SEQS, S_HIST, 4 * P)
    state_p = out["out_state_p"].transpose(0, 2, 1, 3)[:, None]
    state_s = out["out_state_s"].transpose(0, 2, 3, 1, 4)
    return (y[None, :N_PROMPT], y[N_PROMPT:].reshape(SEQS, SEQ_T, D_MODEL), state_p, new_g[:, :1], new_s[:, :1],
            state_s, new_g[:, 1:], new_s[:, 1:])
```
